# Optimizing a Trainium2 kernel written in Bass

```python
import math
import jax, jax.numpy as jnp
from jax import lax
import numpy as np

D_MODEL = 2048
BATCH = 1
SEQ = 256
DEPTH = 1

HEAD_DIM = 128
MIX_WIDTH = D_MODEL
N_HEADS_DIFF = MIX_WIDTH // (2 * HEAD_DIM)
N_HEADS_DIL = MIX_WIDTH // (2 * HEAD_DIM)
DIFF_QK_DIM = HEAD_DIM // 2
DIFF_WIDTH = N_HEADS_DIFF * HEAD_DIM
DIL_WIDTH = N_HEADS_DIL * HEAD_DIM
IN_COLS = 3 * DIFF_WIDTH + 3 * DIL_WIDTH
D_FF = 4 * D_MODEL
DILATION_CONFIGS = ((128, 1), (512, 4), (2048, 16))
BLOCK = 128
ROPE_THETA = 10000.0
LN_EPS = 1e-5
SUBLN_EPS = 1e-5
NEG = -1e30
DEEPNORM_ALPHA = (2.0 * DEPTH) ** 0.25
DEEPNORM_BETA = (8.0 * DEPTH) ** -0.25

kernel_name = "hymba_diffattn_dilated_sqrelu_deepnorm"

def rope_tables(seq, dim):
    inv = 1.0 / (ROPE_THETA ** (jnp.arange(0, dim, 2, dtype=jnp.float32) / dim))
    ang = jnp.arange(seq, dtype=jnp.float32)[:, None] * inv[None, :]
    ang = jnp.concatenate([ang, ang], axis=-1)
    return jnp.cos(ang), jnp.sin(ang)

def apply_rope(x, cos, sin):
    half = x.shape[-1] // 2
    rot = jnp.concatenate([-x[..., half:], x[..., :half]], axis=-1)
    shape = (1, cos.shape[0]) + (1,) * (x.ndim - 3) + (cos.shape[1],)
    return x * cos.reshape(shape) + rot * sin.reshape(shape)

def layer_norm(x, g, b):
    xf = x.astype(jnp.float32)
    mu = jnp.mean(xf, axis=-1, keepdims=True)
    var = jnp.mean(jnp.square(xf - mu), axis=-1, keepdims=True)
    y = (xf - mu) * lax.rsqrt(var + LN_EPS) * g.astype(jnp.float32) + b.astype(jnp.float32)
    return y.astype(x.dtype)

def diff_attention(q, k, v, lam, subln_g, lambda_init):
    B, S, H, _, Dqk = q.shape
    nb = S // BLOCK
    scale = Dqk ** -0.5
    qb = q.reshape(B, nb, BLOCK, H, 2, Dqk).transpose(1, 0, 2, 3, 4, 5)
    k_pos = jnp.arange(S)

    def one_block(args):
        qi, i = args
        s = jnp.einsum('bqhmd,bkhmd->bhmqk', qi, k) * scale
        q_pos = i * BLOCK + jnp.arange(BLOCK)
        causal = k_pos[None, :] <= q_pos[:, None]
        p = jax.nn.softmax(jnp.where(causal, s, NEG), axis=-1)
        a = p[:, :, 0] - lam * p[:, :, 1]
        return jnp.einsum('bhqk,bkhd->bqhd', a, v)

    o = lax.map(one_block, (qb, jnp.arange(nb)))
    o = o.transpose(1, 0, 2, 3, 4).reshape(B, S, H, v.shape[-1])
    o = o * lax.rsqrt(jnp.mean(o * o, axis=-1, keepdims=True) + SUBLN_EPS) * subln_g.astype(jnp.float32)
    return o * (1.0 - lambda_init)

def dilated_window_attention(q, k, v, window, dilation):
    B, S, H, D = q.shape
    steps = window // dilation
    L = S // dilation
    Lp = ((L + BLOCK - 1) // BLOCK) * BLOCK
    nb = Lp // BLOCK

    def to_sub(t):
        t = t.reshape(B, L, dilation, H, D).transpose(0, 2, 3, 1, 4)
        t = jnp.pad(t, ((0, 0), (0, 0), (0, 0), (0, Lp - L), (0, 0)))
        return t.reshape(B, dilation, H, nb, BLOCK, D)

    qb, kb, vb = to_sub(q), to_sub(k), to_sub(v)
    pad_prev = ((0, 0), (0, 0), (0, 0), (1, 0), (0, 0), (0, 0))
    kwin = jnp.concatenate([jnp.pad(kb[:, :, :, :-1], pad_prev), kb], axis=4)
    vwin = jnp.concatenate([jnp.pad(vb[:, :, :, :-1], pad_prev), vb], axis=4)

    s = jnp.einsum('brhnqd,brhnkd->brhnqk', qb, kwin) * (D ** -0.5)
    qi = jnp.arange(BLOCK)[:, None]
    kj = jnp.arange(2 * BLOCK)[None, :]
    dist = qi + BLOCK - kj
    band = (dist >= 0) & (dist <= steps)
    key_exists = (jnp.arange(nb)[:, None, None] * BLOCK + kj[None] - BLOCK) >= 0
    mask = band[None] & key_exists
    s = jnp.where(mask, s, NEG)
    m = jnp.max(s, axis=-1, keepdims=True)
    e = jnp.exp(s - m)
    l = jnp.sum(e, axis=-1, keepdims=True)
    o = jnp.einsum('brhnqk,brhnkd->brhnqd', e, vwin) / l
    lse = m + jnp.log(l)

    def from_sub(t):
        c = t.shape[-1]
        t = t.reshape(B, dilation, H, Lp, c)[:, :, :, :L]
        return t.transpose(0, 3, 1, 2, 4).reshape(B, S, H, c)

    return from_sub(o), from_sub(lse)

def dilated_attention(q, k, v):
    outs, lses = [], []
    for window, dilation in DILATION_CONFIGS:
        o, lse = dilated_window_attention(q, k, v, window, dilation)
        outs.append(o)
        lses.append(lse)
    w = jax.nn.softmax(jnp.stack(lses, axis=0), axis=0)
    return jnp.sum(w * jnp.stack(outs, axis=0), axis=0)

def setup_inputs(seed: int = 0) -> dict:
    key = jax.random.key(seed)
    ks = jax.random.split(key, 16)
    f32 = jnp.float32
    x = jax.random.normal(ks[0], (BATCH, SEQ, D_MODEL), f32)
    w_in = jax.random.normal(ks[1], (DEPTH, D_MODEL, IN_COLS), f32) * D_MODEL ** -0.5
    col_scale = jnp.concatenate([
        jnp.ones((2 * DIFF_WIDTH,), f32), jnp.full((DIFF_WIDTH,), DEEPNORM_BETA, f32),
        jnp.ones((2 * DIL_WIDTH,), f32), jnp.full((DIL_WIDTH,), DEEPNORM_BETA, f32)])
    w_in = w_in * col_scale
    lambda_q1 = 0.1 * jax.random.normal(ks[2], (DEPTH, DIFF_QK_DIM), f32)
    lambda_k1 = 0.1 * jax.random.normal(ks[3], (DEPTH, DIFF_QK_DIM), f32)
    lambda_q2 = 0.1 * jax.random.normal(ks[4], (DEPTH, DIFF_QK_DIM), f32)
    lambda_k2 = 0.1 * jax.random.normal(ks[5], (DEPTH, DIFF_QK_DIM), f32)
    subln_g = 1.0 + 0.02 * jax.random.normal(ks[6], (DEPTH, HEAD_DIM), f32)
    w_out = jax.random.normal(ks[7], (DEPTH, MIX_WIDTH, D_MODEL), f32) * (MIX_WIDTH ** -0.5 * DEEPNORM_BETA)
    ln1_g = 1.0 + 0.02 * jax.random.normal(ks[8], (DEPTH, D_MODEL), f32)
    ln1_b = 0.02 * jax.random.normal(ks[9], (DEPTH, D_MODEL), f32)
    w_ff1 = jax.random.normal(ks[10], (DEPTH, D_MODEL, D_FF), f32) * (D_MODEL ** -0.5 * DEEPNORM_BETA)
    w_ff2 = jax.random.normal(ks[11], (DEPTH, D_FF, D_MODEL), f32) * (D_FF ** -0.5 * DEEPNORM_BETA)
    ln2_g = 1.0 + 0.02 * jax.random.normal(ks[12], (DEPTH, D_MODEL), f32)
    ln2_b = 0.02 * jax.random.normal(ks[13], (DEPTH, D_MODEL), f32)
    return {"x": x, "w_in": w_in, "lambda_q1": lambda_q1, "lambda_k1": lambda_k1,
            "lambda_q2": lambda_q2, "lambda_k2": lambda_k2, "subln_g": subln_g,
            "w_out": w_out, "ln1_g": ln1_g, "ln1_b": ln1_b, "w_ff1": w_ff1,
            "w_ff2": w_ff2, "ln2_g": ln2_g, "ln2_b": ln2_b}

def reference(x, w_in, lambda_q1, lambda_k1, lambda_q2, lambda_k2, subln_g, w_out,
              ln1_g, ln1_b, w_ff1, w_ff2, ln2_g, ln2_b):
    B, S, _ = x.shape
    f32 = jnp.float32
    cos_a, sin_a = rope_tables(S, DIFF_QK_DIM)
    cos_b, sin_b = rope_tables(S, HEAD_DIM)
    splits = [DIFF_WIDTH, 2 * DIFF_WIDTH, 3 * DIFF_WIDTH,
              3 * DIFF_WIDTH + DIL_WIDTH, 3 * DIFF_WIDTH + 2 * DIL_WIDTH]
    for l in range(DEPTH):
        lambda_init = 0.8 - 0.6 * math.exp(-0.3 * l)
        proj = jnp.einsum('bsd,dc->bsc', x, w_in[l]).astype(f32)
        q_a, k_a, v_a, q_b, k_b, v_b = jnp.split(proj, splits, axis=-1)
        q_a = apply_rope(q_a.reshape(B, S, N_HEADS_DIFF, 2, DIFF_QK_DIM), cos_a, sin_a)
        k_a = apply_rope(k_a.reshape(B, S, N_HEADS_DIFF, 2, DIFF_QK_DIM), cos_a, sin_a)
        v_a = v_a.reshape(B, S, N_HEADS_DIFF, HEAD_DIM)
        lam = (jnp.exp(jnp.sum(lambda_q1[l].astype(f32) * lambda_k1[l].astype(f32)))
               - jnp.exp(jnp.sum(lambda_q2[l].astype(f32) * lambda_k2[l].astype(f32)))
               + lambda_init)
        o_a = diff_attention(q_a, k_a, v_a, lam, subln_g[l], lambda_init)
        q_b = apply_rope(q_b.reshape(B, S, N_HEADS_DIL, HEAD_DIM), cos_b, sin_b)
        k_b = apply_rope(k_b.reshape(B, S, N_HEADS_DIL, HEAD_DIM), cos_b, sin_b)
        v_b = v_b.reshape(B, S, N_HEADS_DIL, HEAD_DIM)
        o_b = dilated_attention(q_b, k_b, v_b)
        mix = jnp.concatenate([o_a.reshape(B, S, DIFF_WIDTH),
                               o_b.reshape(B, S, DIL_WIDTH)], axis=-1).astype(x.dtype)
        attn_out = jnp.einsum('bsc,cd->bsd', mix, w_out[l])
        x = layer_norm(DEEPNORM_ALPHA * x + attn_out, ln1_g[l], ln1_b[l])
        hdn = jnp.square(jax.nn.relu(jnp.einsum('bsd,df->bsf', x, w_ff1[l])))
        ff_out = jnp.einsum('bsf,fd->bsd', hdn, w_ff2[l])
        x = layer_norm(DEEPNORM_ALPHA * x + ff_out, ln2_g[l], ln2_b[l])
    return x


_drawn_inputs = setup_inputs


def setup_inputs(seed=0):
    import zlib

    import numpy as np

    out = dict(_drawn_inputs(seed))
    spreads = {}
    factors = {'lambda_k2': 6.302,
     'subln_g': 22.287,
     'ln1_g': 7.801,
     'ln1_b': 7.542,
     'ln2_g': 8.483,
     'ln2_b': 8.076}
    for name, (base, spread) in spreads.items():
        noise = np.random.default_rng([zlib.crc32(name.encode()), seed]).standard_normal(out[name].shape)
        drawn = base * np.exp(spread * noise) if base else spread * noise
        out[name] = __import__('jax').numpy.asarray(drawn.astype(out[name].dtype))
    for name, factor in factors.items():
        out[name] = (out[name] * factor).astype(out[name].dtype)
    return out
```

```python
import concourse.bass as bass
import numpy as np
from concourse import mybir

P = 128
F32 = mybir.dt.float32
F32R = mybir.dt.float32r
ALU = mybir.AluOpType
ACT = mybir.ActivationFunctionType
AX = mybir.AxisListType

SEQ, D_MODEL, D_FF, HEAD_DIM = 256, 2048, 8192, 128
TT = SEQ // P
HEADS = D_MODEL // HEAD_DIM
N_DIFF = HEADS // 2
HALF_DIM = HEAD_DIM // 2
KT = D_MODEL // P
KT_FF = D_FF // P
NC = 512
CHUNKS = D_MODEL // NC
CHUNKS_FF = D_FF // NC
KU = 2
SLOTS = 4
UPH = KT // KU
UPF = KT_FF // KU
U_OUT = UPH * HEADS
U_FF1 = U_OUT + UPH * CHUNKS
U_FF2 = U_FF1 + UPH * CHUNKS_FF
U_END = U_FF2 + UPF * CHUNKS
TPC = NC // P

LAMBDA_INIT = 0.8 - 0.6
EPS = 1e-5
ALPHA = 2.0 ** 0.25
NEG = -1e30
ROPE_THETA = 10000.0
DILATION_CONFIGS = ((128, 1), (512, 4), (2048, 16))

KEYS = P + SEQ
T_ID = 0
T_ROPE_A = T_ID + P
T_ROPE_B = T_ROPE_A + 2 * TT * HALF_DIM
T_MASK_A = T_ROPE_B + 2 * TT * HEAD_DIM
T_MASK_B = T_MASK_A + KEYS
T_COLS = T_MASK_B + KEYS


def constant_table():
    table = np.zeros((P, T_COLS), np.float32)
    table[:, T_ID:T_ID + P] = np.eye(P, dtype=np.float32)
    for at, dim in ((T_ROPE_A, HALF_DIM), (T_ROPE_B, HEAD_DIM)):
        exponent = np.arange(0, dim, 2, dtype=np.float32) / np.float32(dim)
        inverse = np.float32(1.0) / np.power(np.float32(ROPE_THETA), exponent)
        angle = (np.arange(SEQ, dtype=np.float32)[:, None] * inverse[None, :]).astype(np.float32)
        cos, sin = np.cos(angle), np.sin(angle)
        whole = np.stack([np.concatenate([cos, cos], 1), np.concatenate([-sin, sin], 1)])
        whole = whole.reshape(2, TT, P, dim).transpose(2, 0, 1, 3)
        table[:, at:at + 2 * TT * dim] = whole.reshape(P, -1)
    t, u = np.arange(SEQ)[:, None], np.arange(SEQ)[None, :]
    causal = u <= t
    count = np.zeros((SEQ, SEQ))
    for window, dilation in DILATION_CONFIGS:
        count += causal & ((t - u) % dilation == 0) & (t - u <= window)
    for at, added in ((T_MASK_A, np.where(causal, 0.0, NEG)),
                      (T_MASK_B, np.where(count > 0, np.log(np.maximum(count, 1)), NEG))):
        table[:, at:at + P] = added[:P, :P]
        table[:, at + P:at + KEYS] = added[P:, :]
    return table


def keys_of(tt):
    return slice(0, P) if tt == 0 else slice(P, KEYS)


def hybrid_layer(nc, x, w_in, lq1, lk1, lq2, lk2, subln_g, w_out, ln1_g, ln1_b, w_ff1, w_ff2,
                 ln2_g, ln2_b, table, out):
    base = -(-nc.sbuf_base // 64) * 64
    KB = 1024

    def at(name, shape, dtype, offset):
        return nc.alloc_sbuf_tensor_at(name, shape, dtype, offset=base + offset)

    w_raw = at("w_raw", [P, SLOTS, KU * NC], F32, 0)
    w_hi = at("w_hi", [P, SLOTS, KU * NC], F32R, 16 * KB)
    w_lo = at("w_lo", [P, SLOTS, KU * NC], F32R, 32 * KB)
    relu = at("relu", [P, TT, NC], F32, 48 * KB)
    small = at("small", [P, 256], F32, 52 * KB)
    ident_t = at("ident_t", [P, P], F32, 53 * KB)
    X0 = 54 * KB
    x1T_hi = at("x1T_hi", [P, KT, SEQ], F32R, X0)
    x1T_lo = at("x1T_lo", [P, KT, SEQ], F32R, X0 + 16 * KB)
    late_hi = at("late_hi", [P, TPC, SEQ], F32R, X0)
    late_lo = at("late_lo", [P, TPC, SEQ], F32R, X0 + 4 * KB)
    y2 = at("y2", [P, TT, D_MODEL], F32, X0 + 8 * KB)
    H0 = X0 + 32 * KB
    EARLY = KT_FF - TPC
    hidT_hi = at("hidT_hi", [P, EARLY, SEQ], F32R, H0)
    hidT_lo = at("hidT_lo", [P, EARLY, SEQ], F32R, H0 + 60 * KB)
    ln2_gb = at("ln2_gb", [P, 2, D_MODEL], F32, H0)
    mixT_hi = at("mixT_hi", [P, HEADS, SEQ], F32R, H0)
    mixT_lo = at("mixT_lo", [P, HEADS, SEQ], F32R, H0 + 16 * KB)
    xT_hi = at("xT_hi", [P, KT, SEQ], F32R, H0 + 32 * KB)
    xT_lo = at("xT_lo", [P, KT, SEQ], F32R, H0 + 48 * KB)
    ln1_gb = at("ln1_gb", [P, 2, D_MODEL], F32, H0 + 64 * KB)
    A0 = H0 + 80 * KB
    tables = at("tables", [P, T_COLS - P], F32, A0)
    rope_cos = at("rope_cos", [P, TT, 2 * P], F32, A0 + 7 * KB)
    rope_sin = at("rope_sin", [P, TT, 2 * P], F32, A0 + 9 * KB)
    qk = at("qk", [P, TT, 2 * P], F32, A0 + 11 * KB)
    qkT = at("qkT", [P, 2, SEQ], F32, A0 + 13 * KB)
    v_sb = at("v_sb", [P, TT, P], F32, A0 + 15 * KB)
    scores = at("scores", [P, 2, KEYS], F32, A0 + 16 * KB)
    probs = at("probs", [P, 2, KEYS], F32, A0 + 19 * KB)
    y1 = at("y1", [P, TT, D_MODEL], F32, A0 + 24 * KB)
    diff_probs = at("diff_probs", [P, KEYS], F32, 48 * KB)
    probsT = at("probsT", [P, KEYS], F32, 48 * KB + 1536)
    o_sb = at("o_sb", [P, TT, P], F32, 48 * KB + 3072)
    squares = at("squares", [P, TT, P], F32, A0 + 22 * KB)

    def part(first, n):
        return small[:, first:first + n]

    neg_max, row_sum, inv_sum = part(0, 4), part(4, 4), part(8, 4)
    diff_scale, sum_sq, o_scale = part(12, 2), part(14, 2), part(16, 2)
    mean_sq, root = part(18, 2), part(20, 2)
    minus_half, subln = part(22, 2), part(24, 1)
    subln_scaled, neg_lam, lam_sum, lam_exp = part(25, 1), part(26, 1), part(28, 2), part(30, 2)
    mean_var, inv_std, neg_mean_std, var_eps = part(32, 4), part(36, 2), part(38, 2), part(40, 2)
    eps_sum = part(42, 2)
    stats = part(48, TT * CHUNKS * 6)
    lam_in = at("lam_in", [P, 4, HALF_DIM], F32, A0 + 23 * KB)
    lam_prod = at("lam_prod", [P, 2, HALF_DIM], F32, H0 + 64 * KB)

    spill = nc.dram_tensor("ln1_spill", [P, TT, D_MODEL], F32).ap()

    def bank(name, first, count):
        return nc.alloc_psum_tensor(name, [P, count, NC], F32)

    proj_ps = [bank("proj_even", 0, TT), bank("proj_odd", 2, TT)]
    acc_ps = proj_ps[0]
    scores_ps = bank("scores_ps", 4, 2)
    turn_ps = bank("turn_ps", 6, 1)
    out_ps = bank("out_ps", 7, 1)
    big_turn = [proj_ps[1], scores_ps]

    sems = {}

    def sem(name):
        sems[name] = nc.alloc_semaphore(name)
        return sems[name]

    w_loaded = [sem(f"w_loaded{s}") for s in range(SLOTS)]
    w_rounded, w_split, w_used = sem("w_rounded"), sem("w_split"), sem("w_used")
    ident_loaded, tables_loaded = sem("ident_loaded"), sem("tables_loaded")
    x_loaded = [sem(f"x_loaded{c}") for c in range(CHUNKS)]
    lam_loaded, gb1_loaded, gb2_loaded = sem("lam_loaded"), sem("gb1_loaded"), sem("gb2_loaded")
    lam_mult, lam_summed, lam_exped, lam_ready = (
        sem("lam_mult"), sem("lam_summed"), sem("lam_exped"), sem("lam_ready"))
    powers_ready = sem("powers_ready")
    turned, turn_rounded, turn_split = sem("turned"), sem("turn_rounded"), sem("turn_split")
    proj_done, v_copied = sem("proj_done"), sem("v_copied")
    rope_terms, roped = sem("rope_terms"), sem("roped")
    qk_turned, qkT_copied = sem("qk_turned"), sem("qkT_copied")
    scores_done, masked, max_found = sem("scores_done"), sem("masked"), sem("max_found")
    exp_done, sum_inverted = sem("exp_done"), sem("sum_inverted")
    diff_scaled, combined = sem("diff_scaled"), sem("combined")
    probs_turned, probsT_copied = sem("probs_turned"), sem("probsT_copied")
    pv_done, squared = sem("pv_done"), sem("squared")
    mean_ready, root_ready, scale_ready = sem("mean_ready"), sem("root_ready"), sem("scale_ready")
    o_ready, o_turned = sem("o_ready"), sem("o_turned")
    mix_rounded, mix_split = sem("mix_rounded"), sem("mix_split")
    out_done, y1_summed, y1_stats = sem("out_done"), sem("y1_summed"), sem("y1_stats")
    moments, var_ready, std_ready, shift_mult, shift_ready = (
        sem("moments"), sem("var_ready"), sem("std_ready"), sem("shift_mult"), sem("shift_ready"))
    normed, scaled, x1_ready, spilled = sem("normed"), sem("scaled"), sem("x1_ready"), sem("spilled")
    ff1_done, relu_done, hid_squared = sem("ff1_done"), sem("relu_done"), sem("hid_squared")
    hid_turned, hid_rounded, hid_split = sem("hid_turned"), sem("hid_rounded"), sem("hid_split")
    x1_back = sem("x1_back")
    ff2_done, y2_summed, y2_stats = sem("ff2_done"), sem("y2_summed"), sem("y2_stats")
    normed2, scaled2, y2_ready, stored = (
        sem("normed2"), sem("scaled2"), sem("y2_ready"), sem("stored"))

    x_d = x.rearrange("b (t p) d -> p (b t) d", p=P)
    out_d = out.rearrange("b (t p) d -> p (b t) d", p=P)
    w_in_d = w_in.rearrange("l (u k p) (g s h d) -> p (l u) k g s h d", k=KU, p=P, g=2, s=3, d=HEAD_DIM)

    def by_unit(w):
        return w.rearrange("l (u k p) (c n) -> p (l u) k c n", k=KU, p=P, n=NC)

    w_out_d, w_ff1_d, w_ff2_d = by_unit(w_out), by_unit(w_ff1), by_unit(w_ff2)

    def one(i):
        return bass.ds(i, 1)

    HC = 3 * HEAD_DIM

    def load_head_unit(sp, kind, h, head, k, first_lap=False):
        slot = k % SLOTS
        if not first_lap:
            sp.wait_ge(w_split, UPH * h + k - (SLOTS - 1))
        dst = w_raw[:, slot, 0:KU * HC].rearrange("p (k s d) -> p k s d", k=KU, s=3)
        for kk in range(KU):
            src = w_in_d[:, k, kk, kind, :, one(head), :].rearrange("p s h d -> p s (h d)")
            sp.dma_start(dst[:, kk], src).then_inc(w_loaded[slot], 16)

    def load_chunk_unit(sp, w, u, row, chunk, slot):
        sp.wait_ge(w_split, u - (SLOTS - 1))
        dst = w_raw[:, slot, :].rearrange("p (k n) -> p k n", k=KU)
        src = w[:, row, :, chunk, :] if isinstance(chunk, int) else (
            w[:, row, :, one(chunk), :].rearrange("p k c n -> p k (c n)"))
        sp.dma_start(dst, src).then_inc(w_loaded[slot], 16)

    def sync_program(sp):
        for k in range(UPH):
            if k < CHUNKS:
                cols = slice(k * NC, (k + 1) * NC)
                sp.dma_start(y1[:, :, cols], x_d[:, :, cols]).then_inc(x_loaded[k], 16)
            load_head_unit(sp, 0, 0, 0, k, first_lap=k < SLOTS)
        for kind in range(2):
            first = 1 if kind == 0 else 0
            with sp.Fori(first, N_DIFF) as j:
                for k in range(UPH):
                    load_head_unit(sp, kind, j + N_DIFF * kind, j, k)
        with sp.Fori(0, CHUNKS) as n:
            for k in range(UPH):
                load_chunk_unit(sp, w_out_d, UPH * n + (U_OUT + k), k, n, k % SLOTS)
        with sp.Fori(0, CHUNKS_FF) as n:
            for k in range(UPH):
                load_chunk_unit(sp, w_ff1_d, UPH * n + (U_FF1 + k), k, n, k % SLOTS)
        with sp.Fori(0, CHUNKS - 1) as n:
            with sp.Fori(0, UPF // SLOTS) as lap:
                for k in range(SLOTS):
                    load_ff2_unit(sp, UPF * n + SLOTS * lap + (U_FF2 + k), SLOTS * lap + k, n, k)
        for k in range(UPF):
            load_ff2_unit(sp, U_FF2 + UPF * (CHUNKS - 1) + k, k, CHUNKS - 1, k % SLOTS)
            if k == UPF * 3 // 4:
                sp.wait_ge(w_used, U_FF2 + UPF * (CHUNKS - 1) + UPF // 2)
                for n, v in enumerate((ln2_g, ln2_b)):
                    sp.dma_start(ln2_gb[:, n, :], v.partition_broadcast(P).rearrange(
                        "p l d -> p (l d)")).then_inc(gb2_loaded, 16)
        for c in range(CHUNKS):
            cols = slice(c * NC, (c + 1) * NC)
            sp.wait_ge(y2_ready, c + 1)
            sp.dma_start(out_d[:, :, cols], y2[:, :, cols]).then_inc(stored, 16)
        sp.wait_ge(stored, 16 * CHUNKS)

    def load_ff2_unit(sp, u, row, chunk, slot):
        sp.wait_ge(w_split, u - (SLOTS - 1))
        dst = w_raw[:, slot, :].rearrange("p (k n) -> p k n", k=KU)
        if isinstance(row, int):
            src = w_ff2_d[:, row, :, chunk, :]
        else:
            src = w_ff2_d[:, one(row), :, one(chunk), :].rearrange("p u k c n -> p (u k) (c n)")
        sp.dma_start(dst, src).then_inc(w_loaded[slot], 16)

    def tensor_program(pe):
        def transpose_chunk(c, source, ready, value):
            pe.wait_ge(ready, value)
            dst = big_turn[c % 2].rearrange("p b n -> p (b n)")
            for t in range(TPC):
                for tt in range(TT):
                    k = c * TPC + t
                    ins = pe.transpose(dst[:, t * SEQ + tt * P:t * SEQ + (tt + 1) * P],
                                       source[:, tt, k * P:(k + 1) * P], ident_t[:, :])
            ins.then_inc(turned, 1)

        def products(u, k0, slot, left_hi, left_lo, acc, cols, kts, tok_done=None, wait_acc=None):
            pe.wait_ge(w_split, u + 1)
            for tt in range(TT):
                if wait_acc is not None:
                    wait_acc(tt)
                toks = slice(tt * P, (tt + 1) * P)
                for kk in range(KU):
                    k = k0 + kk
                    hi, lo = left_hi(k), left_lo(k)
                    w = slice(kk * cols, (kk + 1) * cols)
                    pe.matmul(acc[:, tt, 0:cols], hi[:, toks], w_hi[:, slot, w],
                              start=(k == 0), stop=False)
                    pe.matmul(acc[:, tt, 0:cols], hi[:, toks], w_lo[:, slot, w],
                              start=False, stop=False)
                    ins = pe.matmul(acc[:, tt, 0:cols], lo[:, toks], w_hi[:, slot, w],
                                    start=False, stop=(k == kts - 1))
                if tt == TT - 1:
                    ins.then_inc(w_used, 1)
                elif tok_done is not None:
                    ins.then_inc(tok_done, 1)

        def turn_qk(h):
            pe.wait_ge(roped, h + 1)
            for s in range(2):
                for tt in range(TT):
                    ins = pe.transpose(turn_ps[:, 0, s * SEQ + tt * P:s * SEQ + (tt + 1) * P],
                                       qk[:, tt, s * P:(s + 1) * P], ident_t[:, :])
            ins.then_inc(qk_turned, 1)

        def score(h, maps):
            pe.wait_ge(qkT_copied, h + 1)
            width = P // maps
            for m in range(maps):
                rows = slice(m * width, (m + 1) * width)
                for tt in range(TT):
                    ins = pe.matmul(scores_ps[:, m, keys_of(tt)], qkT[rows, 0, tt * P:(tt + 1) * P],
                                    qkT[rows, 1, 0:(tt + 1) * P], start=True, stop=True)
            ins.then_inc(scores_done, 1)

        def turn_probs(h, maps):
            if maps == 2:
                pe.wait_ge(combined, h + 1)
            else:
                pe.wait_ge(exp_done, h + 1)
            if not (isinstance(h, int) and h == 0):
                pe.wait_ge(mix_split, h)
            source = diff_probs if maps == 2 else probs[:, 0, :]
            for b in range(3):
                ins = pe.transpose(out_ps[:, 0, b * P:(b + 1) * P], source[:, b * P:(b + 1) * P],
                                   ident_t[:, :])
            ins.then_inc(probs_turned, 1)

        def weigh_values(h):
            pe.wait_ge(probsT_copied, h + 1)
            pe.matmul(out_ps[:, 0, 0:P], probsT[:, 0:P], v_sb[:, 0, :], start=True, stop=True)
            pe.matmul(out_ps[:, 0, P:2 * P], probsT[:, P:2 * P], v_sb[:, 0, :], start=True, stop=False)
            pe.matmul(out_ps[:, 0, P:2 * P], probsT[:, 2 * P:3 * P], v_sb[:, 1, :],
                      start=False, stop=True).then_inc(pv_done, 1)

        def turn_output(h):
            pe.wait_ge(o_ready, h + 1)
            for tt in range(TT):
                ins = pe.transpose(out_ps[:, 0, SEQ + tt * P:SEQ + (tt + 1) * P], o_sb[:, tt, :],
                                   ident_t[:, :])
            ins.then_inc(o_turned, 1)

        def slot(h, parity, att_maps, has_out, unit):
            for k in range(UPH):
                unit(k)
                if k == 0 and has_out:
                    turn_output(h - 2)
                if k == 1 and att_maps:
                    turn_qk(h - 1)
                if k == 2 and att_maps:
                    score(h - 1, att_maps)
                if k == 5 and att_maps:
                    turn_probs(h - 1, att_maps)
                if k == 6 and att_maps:
                    weigh_values(h - 1)

        def head_slot(h, parity, att_maps, has_out):
            acc = proj_ps[parity]

            def unit(k):
                if k == 0 and not (isinstance(h, int) and h < 2):
                    pe.wait_ge(roped, h - 1)
                if isinstance(h, int) and h == 0:
                    for c in {0: (0, 1), 2: (2,), 4: (3,)}.get(k, ()):
                        if c >= 2:
                            pe.wait_ge(turn_split, c - 1)
                        transpose_chunk(c, y1, x_loaded[c], 16)
                    pe.wait_ge(turn_split, k * KU // TPC + 1)
                products(UPH * h + k, KU * k, k % SLOTS, lambda i: xT_hi[:, i, :],
                         lambda i: xT_lo[:, i, :], acc, HC, KT)

            slot(h, parity, att_maps, has_out, unit)
        pe.wait_ge(ident_loaded, 16)
        head_slot(0, 0, 0, False)
        head_slot(1, 1, 2, False)
        with pe.Fori(1, N_DIFF // 2) as j:
            head_slot(2 * j, 0, 2, True)
            head_slot(2 * j + 1, 1, 2, True)
        head_slot(N_DIFF, 0, 2, True)
        head_slot(N_DIFF + 1, 1, 1, True)
        with pe.Fori(N_DIFF // 2 + 1, HEADS // 2) as j:
            head_slot(2 * j, 0, 1, True)
            head_slot(2 * j + 1, 1, 1, True)

        def out_unit(n, k):
            def free(tt):
                if k == 0:
                    if isinstance(n, int) and n == 0:
                        pe.wait_ge(roped, HEADS - 1)
                    else:
                        pe.wait_ge(y1_summed, TT * n - TT + tt + 1)
            products(UPH * n + (U_OUT + k), KU * k, k % SLOTS, lambda i: mixT_hi[:, i, :],
                     lambda i: mixT_lo[:, i, :], acc_ps, NC, KT,
                     tok_done=out_done if k == UPH - 1 else None, wait_acc=free)

        for k in range(UPH):
            if k == UPH - 1:
                turn_output(HEADS - 1)
                pe.wait_ge(mix_split, HEADS)
            out_unit(0, k)
            if k == 0:
                turn_output(HEADS - 2)
                turn_qk(HEADS - 1)
            if k == 1:
                score(HEADS - 1, 1)
            if k == 4:
                turn_probs(HEADS - 1, 1)
            if k == 5:
                weigh_values(HEADS - 1)
        with pe.Fori(1, CHUNKS) as n:
            for k in range(UPH):
                out_unit(n, k)

        def ff1_unit(i, k):
            def free(tt):
                if k == 0:
                    if isinstance(i, int) and i == 0:
                        pe.wait_ge(y1_summed, TT * CHUNKS - TT + tt + 1)
                    else:
                        pe.wait_ge(relu_done, TT * i - TT + tt + 1)
            products(UPH * i + (U_FF1 + k), KU * k, k % SLOTS, lambda t: x1T_hi[:, t, :],
                     lambda t: x1T_lo[:, t, :], acc_ps, NC, KT,
                     tok_done=ff1_done if k == UPH - 1 else None, wait_acc=free)

        def turn_hidden(i):
            pe.wait_ge(hid_squared, i + 1)
            dst = scores_ps.rearrange("p b n -> p (b n)")
            for t in range(TPC):
                for tt in range(TT):
                    ins = pe.transpose(dst[:, t * SEQ + tt * P:t * SEQ + (tt + 1) * P],
                                       relu[:, tt, t * P:(t + 1) * P], ident_t[:, :])
            ins.then_inc(hid_turned, 1)

        for k in range(UPH):
            if k in (0, 2, 3, 4):
                c = max(k - 1, 0)
                if c >= 2:
                    pe.wait_ge(turn_split, CHUNKS + c - 1)
                transpose_chunk(c, y1, x1_ready, c + 1)
            pe.wait_ge(turn_split, CHUNKS + k * KU // TPC + 1)
            ff1_unit(0, k)
        with pe.Fori(1, CHUNKS_FF) as i:
            for k in range(UPH):
                ff1_unit(i, k)
                if k == 1:
                    turn_hidden(i - 1)

        def hid(early, late):
            return lambda t: early[:, t, :] if t < EARLY else late[:, t - EARLY, :]

        def ff2_chunk(n):
            for k in range(UPF):
                def free(tt, k=k):
                    if k == 0:
                        if isinstance(n, int) and n == 0:
                            pe.wait_ge(relu_done, TT * CHUNKS_FF - TT + tt + 1)
                        else:
                            pe.wait_ge(y2_summed, TT * n - TT + tt + 1)
                products(UPF * n + (U_FF2 + k), KU * k, k % SLOTS, hid(hidT_hi, late_hi),
                         hid(hidT_lo, late_lo), acc_ps, NC, KT_FF,
                         tok_done=ff2_done if k == UPF - 1 else None, wait_acc=free)
                if isinstance(n, int) and n == 0 and k == 1:
                    turn_hidden(CHUNKS_FF - 1)
                if isinstance(n, int) and n == 0 and k == UPF - 3:
                    pe.wait_ge(hid_split, CHUNKS_FF)

        ff2_chunk(0)
        with pe.Fori(1, CHUNKS) as n:
            ff2_chunk(n)

    def scalar_program(act):
        def round_unit(u, slot, lap, cols, fresh=False):
            if cols == KU * HC:
                loads = KU * lap
            else:
                loads = lap + (KU - 1) * (U_OUT // SLOTS)
            act.wait_ge(w_loaded[slot], 16 * loads)
            if not fresh:
                act.wait_ge(w_used, u - (SLOTS - 1))
            act.activation(w_hi[:, slot, 0:cols], w_raw[:, slot, 0:cols], ACT.Copy).then_inc(
                w_rounded, 1)

        def ahead(first, k, cols=KU * NC):
            laps = first_lap(first)
            round_unit(first + (k + SLOTS), k % SLOTS, laps + (k // SLOTS + 2), cols)

        def round_turned(c, hi):
            act.wait_ge(turned, c + 1)
            src = big_turn[c % 2].rearrange("p b n -> p (b n)")
            act.activation(hi.rearrange("p k t -> p (k t)"), src, ACT.Copy).then_inc(turn_rounded, 1)

        def copy_v(h, parity):
            act.wait_ge(w_used, UPH * h + UPH)
            act.activation(v_sb[:, :, :], proj_ps[parity][:, :, 2 * P:3 * P], ACT.Copy).then_inc(
                v_copied, 1)

        def copy_qkT(h):
            act.wait_ge(qk_turned, h + 1)
            act.activation(qkT[:, :, :].rearrange("p s t -> p (s t)"), turn_ps[:, 0, :],
                           ACT.Copy).then_inc(qkT_copied, 1)

        def exponentials(h, maps):
            act.wait_ge(max_found, 2 * h + 2)
            for tt in range(TT):
                for m in range(maps):
                    i = 2 * tt + m
                    ins = act.activation(probs[:, m, keys_of(tt)], scores[:, m, keys_of(tt)], ACT.Exp,
                                         bias=neg_max[:, i:i + 1], accum_out=row_sum[:, i:i + 1])
            ins.then_inc(exp_done, 1)

        def copy_probsT(h):
            act.wait_ge(probs_turned, h + 1)
            act.activation(probsT[:, :], out_ps[:, 0, 0:KEYS], ACT.Copy).then_inc(probsT_copied, 1)

        def square_sums(h):
            act.wait_ge(pv_done, h + 1)
            act.wait_ge(sum_inverted, h + 1)
            for tt in range(TT):
                ins = act.activation(squares[:, tt, :], out_ps[:, 0, tt * P:(tt + 1) * P], ACT.Square,
                                     scale=inv_sum[:, 2 * tt:2 * tt + 1],
                                     accum_out=sum_sq[:, tt:tt + 1])
            ins.then_inc(squared, 1)

        def scale_output(h, maps):
            if maps == 2:
                act.wait_ge(scale_ready, h + 1)
            else:
                act.wait_ge(pv_done, h + 1)
                act.wait_ge(sum_inverted, h + 1)
            for tt in range(TT):
                by = o_scale[:, tt:tt + 1] if maps == 2 else inv_sum[:, 2 * tt:2 * tt + 1]
                ins = act.activation(o_sb[:, tt, :], out_ps[:, 0, tt * P:(tt + 1) * P], ACT.Copy,
                                     scale=by)
            ins.then_inc(o_ready, 1)

        def round_mix(h, maps):
            act.wait_ge(o_turned, h + 1)
            dst = mixT_hi[:, h, :] if isinstance(h, int) else (
                mixT_hi[:, one(h), :].rearrange("p h t -> p (h t)"))
            act.activation(dst, out_ps[:, 0, SEQ:2 * SEQ], ACT.Copy,
                           scale=subln_scaled if maps == 2 else 1.0).then_inc(mix_rounded, 1)

        def slot(h, parity, att_maps, out_maps, columns=None):
            cols = columns or KU * HC
            first = UPH * h
            if att_maps:
                copy_v(h - 1, 1 - parity)
            ahead(first, 0, cols)
            if out_maps:
                round_mix(h - 2, out_maps)
            ahead(first, 1, cols)
            if att_maps:
                copy_qkT(h - 1)
            ahead(first, 2, cols)
            if att_maps:
                exponentials(h - 1, att_maps)
            ahead(first, 3, cols)
            cols = KU * NC if isinstance(h, int) and h == HEADS - 1 else cols
            ahead(first, 4, cols)
            ahead(first, 5, cols)
            if att_maps:
                copy_probsT(h - 1)
            ahead(first, 6, cols)
            if att_maps == 2:
                square_sums(h - 1)
            ahead(first, 7, cols)
            if att_maps:
                scale_output(h - 1, att_maps)

        for c in range(SLOTS):
            round_unit(c, c, 1, KU * HC, fresh=True)
            if c == 0:
                act.wait_ge(lam_loaded, 16 * 5)
                act.activation(subln_scaled, subln, ACT.Copy,
                               scale=(1.0 - LAMBDA_INIT) * HEAD_DIM ** 0.5)
                act.wait_ge(lam_summed, 2)
                act.activation(lam_exp, lam_sum, ACT.Exp).then_inc(lam_exped, 1)
            round_turned(c, xT_hi[:, c * TPC:(c + 1) * TPC, :])
        slot(0, 0, 0, 0)
        slot(1, 1, 2, 0)
        with act.Fori(1, N_DIFF // 2) as j:
            slot(2 * j, 0, 2, 2)
            slot(2 * j + 1, 1, 2, 2)
        slot(N_DIFF, 0, 2, 2)
        slot(N_DIFF + 1, 1, 1, 2)
        with act.Fori(N_DIFF // 2 + 1, HEADS // 2 - 1) as j:
            slot(2 * j, 0, 1, 1)
            slot(2 * j + 1, 1, 1, 1)
        slot(HEADS - 2, 0, 1, 1)
        slot(HEADS - 1, 1, 1, 1)

        copy_v(HEADS - 1, 1)
        round_mix(HEADS - 2, 1)
        ahead(U_OUT, 0)
        copy_qkT(HEADS - 1)
        ahead(U_OUT, 1)
        ahead(U_OUT, 2)
        exponentials(HEADS - 1, 1)
        ahead(U_OUT, 3)
        ahead(U_OUT, 4)
        copy_probsT(HEADS - 1)
        ahead(U_OUT, 5)
        scale_output(HEADS - 1, 1)
        round_mix(HEADS - 1, 1)
        ahead(U_OUT, 6)
        ahead(U_OUT, 7)
        with act.Fori(1, CHUNKS) as n:
            for k in range(UPH):
                ahead(UPH * n + U_OUT, k)

        act.wait_ge(shift_ready, 1)
        for c in range(CHUNKS):
            for tt in range(TT):
                cols = slice(c * NC, (c + 1) * NC)
                act.activation(y1[:, tt, cols], y1[:, tt, cols], ACT.Identity,
                               bias=neg_mean_std[:, tt:tt + 1],
                               scale=inv_std[:, tt:tt + 1]).then_inc(normed, 1)
            if c >= 1:
                round_turned(CHUNKS + c - 1, x1T_hi[:, (c - 1) * TPC:c * TPC, :])
            if c >= 2:
                ahead(U_FF1, c - 2)
        round_turned(2 * CHUNKS - 1, x1T_hi[:, (CHUNKS - 1) * TPC:, :])

        def relu_chunk(i):
            for tt in range(TT):
                if tt == 0:
                    act.wait_ge(ff1_done, i + 1)
                else:
                    act.wait_ge(w_used, UPH * i + (U_FF1 + UPH))
                if not (isinstance(i, int) and i == 0):
                    act.wait_ge(hid_turned, i)
                act.activation(relu[:, tt, :], acc_ps[:, tt, :], ACT.Relu).then_inc(relu_done, 1)

        def round_hidden(i, last=False):
            act.wait_ge(hid_turned, i + 1)
            dst = late_hi if last else hidT_hi[:, bass.ds(i * TPC, TPC), :]
            act.activation(dst.rearrange("p k t -> p (k t)"),
                           scores_ps.rearrange("p b n -> p (b n)"), ACT.Copy).then_inc(hid_rounded, 1)

        def ff1_slot(i, first, begin=0):
            for k in range(begin, UPH):
                if k == 2 and not (isinstance(i, int) and i == 0):
                    round_hidden(i - 1)
                if k == UPH - 1:
                    relu_chunk(i)
                ahead(first, k)

        ff1_slot(0, U_FF1, begin=2)
        with act.Fori(1, CHUNKS_FF) as i:
            ff1_slot(i, UPH * i + U_FF1)

        for k in range(SLOTS):
            if k == 2:
                round_hidden(CHUNKS_FF - 1, last=True)
            ahead(U_FF2, k)
        with act.Fori(1, (U_END - U_FF2) // SLOTS - 1) as lap:
            for k in range(SLOTS):
                ahead(SLOTS * lap + U_FF2, k)
        act.wait_ge(shift_ready, 2)
        for c in range(CHUNKS):
            for tt in range(TT):
                cols = slice(c * NC, (c + 1) * NC)
                act.activation(y2[:, tt, cols], y2[:, tt, cols], ACT.Identity,
                               bias=neg_mean_std[:, tt:tt + 1],
                               scale=inv_std[:, tt:tt + 1]).then_inc(normed2, 1)

    def first_lap(first):
        return first // SLOTS if isinstance(first, int) else first // SLOTS

    def vector_program(dve):
        def split_unit(u, slot, cols):
            dve.wait_ge(w_rounded, u + 1)
            dve.tensor_tensor(w_lo[:, slot, 0:cols], w_raw[:, slot, 0:cols],
                              w_hi[:, slot, 0:cols].bitcast(F32), ALU.subtract).then_inc(w_split, 1)

        def ahead(first, k, cols=KU * NC):
            split_unit(first + (k + SLOTS), k % SLOTS, cols)

        def split_turned(c, hi, lo):
            dve.wait_ge(turn_rounded, c + 1)
            src = big_turn[c % 2].rearrange("p b n -> p (b n)")
            dve.tensor_tensor(lo.rearrange("p k t -> p (k t)"), src,
                              hi.rearrange("p k t -> p (k t)").bitcast(F32),
                              ALU.subtract).then_inc(turn_split, 1)

        def rope(h, parity, maps):
            width = P // maps
            half = width // 2
            groups = 2 * maps
            t0 = (T_ROPE_A if maps == 2 else T_ROPE_B) - P
            tabs = tables[:, t0:t0 + 2 * TT * width].rearrange("p (c t d) -> p c t d", c=2, t=TT)

            def grouped(ap):
                return ap.rearrange("p t (g d) -> p t g d", g=groups)

            def spread(ap):
                return ap.unsqueeze(2).to_broadcast([P, TT, groups, ap.shape[-1]])

            src = grouped(proj_ps[parity][:, :, 0:2 * P])
            sin = tabs[:, 1]
            dve.wait_ge(v_copied, h + 1)
            dve.tensor_tensor(grouped(rope_cos[:, :, :]), src, spread(tabs[:, 0]),
                              ALU.mult).then_inc(rope_terms, 1)
            dve.tensor_tensor(grouped(rope_sin[:, :, :])[:, :, :, 0:half], src[:, :, :, half:width],
                              spread(sin[:, :, 0:half]), ALU.mult).then_inc(rope_terms, 1)
            dve.tensor_tensor(grouped(rope_sin[:, :, :])[:, :, :, half:width], src[:, :, :, 0:half],
                              spread(sin[:, :, half:width]), ALU.mult).then_inc(rope_terms, 1)
            dve.wait_ge(rope_terms, 3 * h + 3)
            dve.tensor_tensor(qk[:, :, :], rope_cos[:, :, :], rope_sin[:, :, :],
                              ALU.add).then_inc(roped, 1)

        def mask_and_max(h, maps):
            t0 = (T_MASK_A if maps == 2 else T_MASK_B) - P
            mask = tables[:, t0:t0 + KEYS].unsqueeze(1).to_broadcast([P, maps, KEYS])
            scale = float((P // maps) ** -0.5)
            dve.wait_ge(scores_done, h + 1)
            dve.scalar_tensor_tensor(out=scores[:, 0:maps, :], in0=scores_ps[:, 0:maps, 0:KEYS],
                                     scalar=scale, in1=mask, op0=ALU.mult,
                                     op1=ALU.add).then_inc(masked, 1)
            dve.wait_ge(masked, h + 1)
            for tt in range(TT):
                dve.tensor_reduce(neg_max[:, 2 * tt:2 * tt + maps], scores[:, 0:maps, keys_of(tt)],
                                  AX.X, ALU.max, negate=True).then_inc(max_found, 1)

        def invert_sums(h, maps):
            dve.wait_ge(exp_done, h + 1)
            if maps == 2:
                dve.reciprocal(inv_sum[:, :], row_sum[:, :]).then_inc(sum_inverted, 1)
            else:
                dve.reciprocal(inv_sum[:, 0:4:2], row_sum[:, 0:4:2]).then_inc(sum_inverted, 1)

        def combine(h):
            dve.wait_ge(sum_inverted, h + 1)
            dve.scalar_tensor_tensor(out=diff_scale, in0=row_sum[:, 0:4:2], scalar=neg_lam,
                                     in1=inv_sum[:, 1:4:2], op0=ALU.mult,
                                     op1=ALU.mult).then_inc(diff_scaled, 1)
            dve.wait_ge(diff_scaled, h + 1)
            for tt in range(TT):
                ins = dve.scalar_tensor_tensor(
                    out=diff_probs[:, keys_of(tt)], in0=probs[:, 1, keys_of(tt)],
                    scalar=diff_scale[:, tt:tt + 1], in1=probs[:, 0, keys_of(tt)],
                    op0=ALU.mult, op1=ALU.add)
            ins.then_inc(combined, 1)

        def split_mix(h, maps):
            dve.wait_ge(mix_rounded, h + 1)

            def row(t):
                return t[:, h, :] if isinstance(h, int) else (
                    t[:, one(h), :].rearrange("p h t -> p (h t)"))
            src, hi, lo = out_ps[:, 0, SEQ:2 * SEQ], row(mixT_hi).bitcast(F32), row(mixT_lo)
            if maps == 2:
                dve.scalar_tensor_tensor(out=lo, in0=src, scalar=subln_scaled, in1=hi, op0=ALU.mult,
                                         op1=ALU.subtract).then_inc(mix_split, 1)
            else:
                dve.tensor_tensor(lo, src, hi, ALU.subtract).then_inc(mix_split, 1)

        def slot(h, parity, rope_maps, att_maps, out_maps):
            cols = KU * HC
            first = UPH * h
            if rope_maps:
                rope(h - 1, 1 - parity, rope_maps)
            ahead(first, 0, cols)
            if out_maps:
                split_mix(h - 2, out_maps)
            ahead(first, 1, cols)
            if att_maps:
                mask_and_max(h - 1, att_maps)
            ahead(first, 2, cols)
            ahead(first, 3, cols)
            if att_maps:
                invert_sums(h - 1, att_maps)
            cols = KU * NC if isinstance(h, int) and h == HEADS - 1 else cols
            ahead(first, 4, cols)
            if att_maps == 2:
                combine(h - 1)
            ahead(first, 5, cols)
            ahead(first, 6, cols)
            ahead(first, 7, cols)

        dve.memset(minus_half, -0.5).then_inc(powers_ready, 1)
        dve.memset(eps_sum, HEAD_DIM * EPS).then_inc(powers_ready, 1)
        for c in range(SLOTS):
            split_unit(c, c, KU * HC)
            if c == 0:
                dve.wait_ge(lam_loaded, 16 * 5)
                for n in range(2):
                    dve.tensor_tensor(lam_prod[:, n, :], lam_in[:, 2 * n, :], lam_in[:, 2 * n + 1, :],
                                      ALU.mult).then_inc(lam_mult, 1)
                dve.wait_ge(lam_mult, 2)
                for n in range(2):
                    dve.reduce_sum(lam_sum[:, n:n + 1], lam_prod[:, n, :], AX.X).then_inc(
                        lam_summed, 1)
            split_turned(c, xT_hi[:, c * TPC:(c + 1) * TPC, :], xT_lo[:, c * TPC:(c + 1) * TPC, :])
        dve.wait_ge(lam_exped, 1)
        dve.scalar_tensor_tensor(out=neg_lam, in0=lam_exp[:, 1:2], scalar=LAMBDA_INIT,
                                 in1=lam_exp[:, 0:1], op0=ALU.subtract,
                                 op1=ALU.subtract).then_inc(lam_ready, 1)
        dve.wait_ge(lam_ready, 1)
        dve.wait_ge(tables_loaded, 16)
        slot(0, 0, 0, 0, 0)
        slot(1, 1, 2, 2, 0)
        with dve.Fori(1, N_DIFF // 2) as j:
            slot(2 * j, 0, 2, 2, 2)
            slot(2 * j + 1, 1, 2, 2, 2)
        slot(N_DIFF, 0, 2, 2, 2)
        slot(N_DIFF + 1, 1, 1, 1, 2)
        with dve.Fori(N_DIFF // 2 + 1, HEADS // 2 - 1) as j:
            slot(2 * j, 0, 1, 1, 1)
            slot(2 * j + 1, 1, 1, 1, 1)
        slot(HEADS - 2, 0, 1, 1, 1)
        slot(HEADS - 1, 1, 1, 1, 1)

        def add_residual(n, y, tok_done, end, summed):
            for tt in range(TT):
                if tt == 0:
                    dve.wait_ge(tok_done, n + 1)
                else:
                    dve.wait_ge(w_used, end)
                cols = slice(n * NC, (n + 1) * NC) if isinstance(n, int) else bass.ds(n * NC, NC)
                dve.scalar_tensor_tensor(out=y[:, tt, cols], in0=y[:, tt, cols], scalar=ALPHA,
                                         in1=acc_ps[:, tt, :], op0=ALU.mult,
                                         op1=ALU.add).then_inc(summed, 1)

        def chunk_stats(n, y, summed, stat_done):
            dve.wait_ge(summed, TT * n + TT)
            for tt in range(TT):
                cols = slice(n * NC, (n + 1) * NC) if isinstance(n, int) else bass.ds(n * NC, NC)
                first = tt * CHUNKS * 6 + n * 6
                where = slice(first, first + 6) if isinstance(n, int) else bass.ds(first, 6)
                dve.bn_stats(stats[:, where], y[:, tt, cols]).then_inc(stat_done, 1)

        def find_moments(stat_done):
            dve.wait_ge(stat_done, TT * CHUNKS)
            for tt in range(TT):
                dve.bn_aggr(mean_var[:, 2 * tt:2 * tt + 2],
                            stats[:, tt * CHUNKS * 6:(tt + 1) * CHUNKS * 6]).then_inc(moments, 1)

        rope(HEADS - 1, 1, 1)
        split_mix(HEADS - 2, 1)
        ahead(U_OUT, 0)
        mask_and_max(HEADS - 1, 1)
        ahead(U_OUT, 1)
        ahead(U_OUT, 2)
        ahead(U_OUT, 3)
        invert_sums(HEADS - 1, 1)
        ahead(U_OUT, 4)
        ahead(U_OUT, 5)
        split_mix(HEADS - 1, 1)
        ahead(U_OUT, 6)
        add_residual(0, y1, out_done, U_OUT + UPH, y1_summed)
        ahead(U_OUT, 7)
        chunk_stats(0, y1, y1_summed, y1_stats)
        with dve.Fori(1, CHUNKS) as n:
            for k in range(UPH):
                if k == UPH - 1:
                    add_residual(n, y1, out_done, UPH * n + (U_OUT + UPH), y1_summed)
                    chunk_stats(n, y1, y1_summed, y1_stats)
                ahead(UPH * n + U_OUT, k)
        find_moments(y1_stats)

        def gain_and_offset(c, y, gb, norm_done, scale_done, ready):
            cols = slice(c * NC, (c + 1) * NC)
            dve.wait_ge(norm_done, TT * c + TT)
            dve.tensor_tensor(y[:, :, cols], y[:, :, cols],
                              gb[:, 0, cols].unsqueeze(1).to_broadcast([P, TT, NC]),
                              ALU.mult).then_inc(scale_done, 1)
            dve.wait_ge(scale_done, c + 1)
            dve.tensor_tensor(y[:, :, cols], y[:, :, cols],
                              gb[:, 1, cols].unsqueeze(1).to_broadcast([P, TT, NC]),
                              ALU.add).then_inc(ready, 1)

        dve.wait_ge(gb1_loaded, 32)
        for c in range(CHUNKS):
            gain_and_offset(c, y1, ln1_gb, normed, scaled, x1_ready)
            if c >= 1:
                split_turned(CHUNKS + c - 1, x1T_hi[:, (c - 1) * TPC:c * TPC, :],
                             x1T_lo[:, (c - 1) * TPC:c * TPC, :])
            if c >= 2:
                ahead(U_FF1, c - 2)
        split_turned(2 * CHUNKS - 1, x1T_hi[:, (CHUNKS - 1) * TPC:, :],
                     x1T_lo[:, (CHUNKS - 1) * TPC:, :])

        def square_hidden(i):
            dve.wait_ge(relu_done, TT * i + TT)
            dve.tensor_tensor(relu[:, :, :], relu[:, :, :], relu[:, :, :], ALU.mult).then_inc(
                hid_squared, 1)

        def split_hidden(i, last=False):
            dve.wait_ge(hid_rounded, i + 1)
            hi = late_hi if last else hidT_hi[:, bass.ds(i * TPC, TPC), :]
            lo = late_lo if last else hidT_lo[:, bass.ds(i * TPC, TPC), :]
            dve.tensor_tensor(lo.rearrange("p k t -> p (k t)"),
                              scores_ps.rearrange("p b n -> p (b n)"),
                              hi.rearrange("p k t -> p (k t)").bitcast(F32),
                              ALU.subtract).then_inc(hid_split, 1)

        def ff1_slot(i, first, begin=0):
            for k in range(begin, UPH):
                if k == 2 and not (isinstance(i, int) and i == 0):
                    split_hidden(i - 1)
                ahead(first, k)
            square_hidden(i)

        dve.wait_ge(spilled, 16 * CHUNKS)
        ff1_slot(0, U_FF1, begin=2)
        with dve.Fori(1, CHUNKS_FF) as i:
            ff1_slot(i, UPH * i + U_FF1)

        def ff2_slot(n, first, units):
            with dve.Fori(0, units, SLOTS) as k0:
                for k in range(SLOTS):
                    ahead(first + k0, k)

        for n in range(CHUNKS):
            first = U_FF2 + UPF * n
            if n == 0:
                for k in range(SLOTS):
                    if k == 2:
                        split_hidden(CHUNKS_FF - 1, last=True)
                    ahead(first, k)
            last = n == CHUNKS - 1
            with dve.Fori(SLOTS if n == 0 else 0, UPF - SLOTS, SLOTS) as k0:
                for k in range(SLOTS):
                    ahead(first + k0, k)
            if not last:
                for k in range(SLOTS - 1):
                    ahead(first + UPF - SLOTS, k)
            if n == 0:
                dve.wait_ge(x1_back, 16)
            add_residual(n, y2, ff2_done, first + UPF, y2_summed)
            if not last:
                ahead(first + UPF - SLOTS, SLOTS - 1)
            chunk_stats(n, y2, y2_summed, y2_stats)
        find_moments(y2_stats)
        dve.wait_ge(gb2_loaded, 32)
        for c in range(CHUNKS):
            gain_and_offset(c, y2, ln2_gb, normed2, scaled2, y2_ready)

    def gpsimd_program(pool):
        pool.wait_ge(powers_ready, 2)

        def rms_scale(h):
            pool.wait_ge(squared, h + 1)
            pool.tensor_tensor(mean_sq, sum_sq, eps_sum, ALU.add).then_inc(mean_ready, 1)
            pool.wait_ge(mean_ready, h + 1)
            pool.tensor_tensor(root, mean_sq, minus_half, ALU.pow).then_inc(root_ready, 1)
            pool.wait_ge(root_ready, h + 1)
            pool.tensor_tensor(o_scale, root, inv_sum[:, 0:4:2], ALU.mult).then_inc(scale_ready, 1)

        def norm_scale(n):
            pool.wait_ge(moments, TT * n + TT)
            pool.tensor_scalar(var_eps, mean_var[:, 1:4:2], EPS, None, ALU.add).then_inc(
                var_ready, 1)
            pool.wait_ge(var_ready, n + 1)
            pool.tensor_tensor(inv_std, var_eps, minus_half, ALU.pow).then_inc(std_ready, 1)
            pool.wait_ge(std_ready, n + 1)
            pool.tensor_tensor(neg_mean_std, inv_std, mean_var[:, 0:4:2], ALU.mult).then_inc(
                shift_mult, 1)
            pool.wait_ge(shift_mult, n + 1)
            pool.tensor_scalar(neg_mean_std, neg_mean_std, -1.0, None, ALU.mult).then_inc(
                shift_ready, 1)

        for n, v in enumerate((lq1, lk1, lq2, lk2)):
            pool.dma_start(lam_in[:, n, :], v.partition_broadcast(P).rearrange(
                "p l d -> p (l d)")).then_inc(lam_loaded, 16)
        pool.dma_start(subln, subln_g.rearrange("l d -> d l")).then_inc(lam_loaded, 16)
        pool.dma_start(tables[:, :], table[:, P:T_COLS]).then_inc(tables_loaded, 16)
        with pool.Fori(0, N_DIFF) as h:
            rms_scale(h)
        for n, v in enumerate((ln1_g, ln1_b)):
            pool.wait_ge(w_used, U_OUT)
            pool.dma_start(ln1_gb[:, n, :], v.partition_broadcast(P).rearrange(
                "p l d -> p (l d)")).then_inc(gb1_loaded, 16)
        norm_scale(0)
        for c in range(CHUNKS):
            cols = slice(c * NC, (c + 1) * NC)
            pool.wait_ge(x1_ready, c + 1)
            pool.dma_start(spill[:, :, cols], y1[:, :, cols]).then_inc(spilled, 16)
        pool.wait_ge(spilled, 16 * CHUNKS)
        pool.wait_ge(w_used, U_FF2)
        pool.dma_start(y2[:, :, :], spill).then_inc(x1_back, 16)
        norm_scale(1)

    with nc.Block() as block:
        @block.sync
        def _(sp):
            sp.dma_start(ident_t[:, :], table[:, 0:P]).then_inc(ident_loaded, 16)
            sync_program(sp)

        @block.tensor
        def _(pe):
            tensor_program(pe)

        @block.scalar
        def _(act):
            scalar_program(act)

        @block.vector
        def _(dve):
            vector_program(dve)

        @block.gpsimd
        def _(pool):
            gpsimd_program(pool)


_INS = ["x", "w_in", "lambda_q1", "lambda_k1", "lambda_q2", "lambda_k2", "subln_g", "w_out",
        "ln1_g", "ln1_b", "w_ff1", "w_ff2", "ln2_g", "ln2_b"]


def kernel(**inputs):
    import concourse.bacc as bacc
    from concourse.bass_utils import run_bass_kernel_spmd

    nc = bacc.Bacc("TRN2", target_bir_lowering=False, num_devices=1)
    arrays = {f"in_{n}": np.ascontiguousarray(inputs[n]) for n in _INS}
    arrays["in_table"] = constant_table()
    args = [nc.dram_tensor(n, a.shape, mybir.dt.from_np(a.dtype), kind="ExternalInput").ap()
            for n, a in arrays.items()]
    out = nc.dram_tensor("out_0", inputs["x"].shape, F32, kind="ExternalOutput").ap()
    hybrid_layer(nc, *args, out)
    result = run_bass_kernel_spmd(nc, [arrays], core_ids=[0])
    return result.results[0]["out_0"]
```

```python
import concourse.bass as bass
import numpy as np
from concourse import mybir

P = 128
F32 = mybir.dt.float32
F32R = mybir.dt.float32r
ALU = mybir.AluOpType
ACT = mybir.ActivationFunctionType
AX = mybir.AxisListType

SEQ, D_MODEL, D_FF, HEAD_DIM = 256, 2048, 8192, 128
TT = SEQ // P
HEADS = D_MODEL // HEAD_DIM
N_DIFF = HEADS // 2
HALF_DIM = HEAD_DIM // 2
KT = D_MODEL // P
KT_FF = D_FF // P
NC = 512
CHUNKS = D_MODEL // NC
CHUNKS_FF = D_FF // NC
KU = 2
SLOTS = 4
UPH = KT // KU
UPF = KT_FF // KU
U_OUT = UPH * HEADS
U_FF1 = U_OUT + UPH * CHUNKS
U_FF2 = U_FF1 + UPH * CHUNKS_FF
U_END = U_FF2 + UPF * CHUNKS
TPC = NC // P

PIECES = [(tt, c) for tt in range(TT) for c in range(CHUNKS)]
LAST_PIECES = [(0, slice(0, 1024)), (0, slice(1024, 2048)),
               (1, slice(0, 1024)), (1, slice(1024, 1536)), (1, slice(1536, 2048))]

LAMBDA_INIT = 0.8 - 0.6
EPS = 1e-5
ALPHA = 2.0 ** 0.25
NEG = -1e30
ROPE_THETA = 10000.0
DILATION_CONFIGS = ((128, 1), (512, 4), (2048, 16))

KEYS = P + SEQ
T_ID = 0
T_ROPE_A = T_ID + P
T_ROPE_B = T_ROPE_A + 2 * TT * HALF_DIM
T_MASK_A = T_ROPE_B + 2 * TT * HEAD_DIM
T_MASK_B = T_MASK_A + KEYS
T_COLS = T_MASK_B + KEYS


def constant_table():
    table = np.zeros((P, T_COLS), np.float32)
    table[:, T_ID:T_ID + P] = np.eye(P, dtype=np.float32)
    for at, dim in ((T_ROPE_A, HALF_DIM), (T_ROPE_B, HEAD_DIM)):
        exponent = np.arange(0, dim, 2, dtype=np.float32) / np.float32(dim)
        inverse = np.float32(1.0) / np.power(np.float32(ROPE_THETA), exponent)
        angle = (np.arange(SEQ, dtype=np.float32)[:, None] * inverse[None, :]).astype(np.float32)
        cos, sin = np.cos(angle), np.sin(angle)
        whole = np.stack([np.concatenate([cos, cos], 1), np.concatenate([-sin, sin], 1)])
        whole = whole.reshape(2, TT, P, dim).transpose(2, 0, 1, 3)
        table[:, at:at + 2 * TT * dim] = whole.reshape(P, -1)
    t, u = np.arange(SEQ)[:, None], np.arange(SEQ)[None, :]
    causal = u <= t
    count = np.zeros((SEQ, SEQ))
    for window, dilation in DILATION_CONFIGS:
        count += causal & ((t - u) % dilation == 0) & (t - u <= window)
    for at, added in ((T_MASK_A, np.where(causal, 0.0, NEG)),
                      (T_MASK_B, np.where(count > 0, np.log(np.maximum(count, 1)), NEG))):
        table[:, at:at + P] = added[:P, :P]
        table[:, at + P:at + KEYS] = added[P:, :]
    return table


def keys_of(tt):
    return slice(0, P) if tt == 0 else slice(P, KEYS)


def hybrid_layer(nc, x, w_in, lq1, lk1, lq2, lk2, subln_g, w_out, ln1_g, ln1_b, w_ff1, w_ff2,
                 ln2_g, ln2_b, table, out):
    base = -(-nc.sbuf_base // 64) * 64
    KB = 1024

    def at(name, shape, dtype, offset):
        return nc.alloc_sbuf_tensor_at(name, shape, dtype, offset=base + offset)

    w_raw = at("w_raw", [P, SLOTS, KU * NC], F32, 0)
    w_hi = at("w_hi", [P, SLOTS, KU * NC], F32R, 16 * KB)
    w_lo = at("w_lo", [P, SLOTS, KU * NC], F32R, 32 * KB)
    relu = at("relu", [P, TT, NC], F32, 48 * KB)
    small = at("small", [P, 256], F32, 52 * KB)
    ident_t = at("ident_t", [P, P], F32, 53 * KB)
    X0 = 54 * KB
    x1T_hi = at("x1T_hi", [P, KT, SEQ], F32R, X0)
    x1T_lo = at("x1T_lo", [P, KT, SEQ], F32R, X0 + 16 * KB)
    late_hi = at("late_hi", [P, TPC, SEQ], F32R, X0)
    late_lo = at("late_lo", [P, TPC, SEQ], F32R, X0 + 4 * KB)
    y2 = at("y2", [P, TT, D_MODEL], F32, X0 + 8 * KB)
    H0 = X0 + 32 * KB
    EARLY = KT_FF - TPC
    hidT_hi = at("hidT_hi", [P, EARLY, SEQ], F32R, H0)
    hidT_lo = at("hidT_lo", [P, EARLY, SEQ], F32R, H0 + 60 * KB)
    ln2_gb = at("ln2_gb", [P, 2, D_MODEL], F32, H0)
    mixT_hi = at("mixT_hi", [P, HEADS, SEQ], F32R, H0)
    mixT_lo = at("mixT_lo", [P, HEADS, SEQ], F32R, H0 + 16 * KB)
    xT_hi = at("xT_hi", [P, KT, SEQ], F32R, H0 + 32 * KB)
    xT_lo = at("xT_lo", [P, KT, SEQ], F32R, H0 + 48 * KB)
    ln1_gb = at("ln1_gb", [P, 2, D_MODEL], F32, H0 + 64 * KB)
    side_hi = at("side_hi", [P, SLOTS, KU * NC], F32R, H0 + 32 * KB)
    side_lo = at("side_lo", [P, SLOTS, KU * NC], F32R, H0 + 48 * KB)
    side_raw = at("side_raw", [P, SLOTS, KU * NC], F32, H0 + 80 * KB)
    A0 = H0 + 80 * KB
    tables = at("tables", [P, T_COLS - P], F32, A0)
    rope_cos = at("rope_cos", [P, TT, 2 * P], F32, A0 + 7 * KB)
    rope_sin = at("rope_sin", [P, TT, 2 * P], F32, A0 + 9 * KB)
    qk = at("qk", [P, TT, 2 * P], F32, A0 + 11 * KB)
    qkT = at("qkT", [P, 2, SEQ], F32, A0 + 13 * KB)
    v_sb = at("v_sb", [P, TT, P], F32, A0 + 15 * KB)
    scores = at("scores", [P, 2, KEYS], F32, A0 + 16 * KB)
    probs = at("probs", [P, 2, KEYS], F32, A0 + 19 * KB)
    y1 = at("y1", [P, TT, D_MODEL], F32, A0 + 24 * KB)
    diff_probs = at("diff_probs", [P, KEYS], F32, 48 * KB)
    probsT = at("probsT", [P, KEYS], F32, 48 * KB + 1536)
    o_sb = at("o_sb", [P, TT, P], F32, 48 * KB + 3072)
    squares = at("squares", [P, TT, P], F32, A0 + 22 * KB)

    def part(first, n):
        return small[:, first:first + n]

    neg_max, row_sum, inv_sum = part(0, 4), part(4, 4), part(8, 4)
    diff_scale, sum_sq, o_scale = part(12, 2), part(14, 2), part(16, 2)
    mean_sq, root = part(18, 2), part(20, 2)
    minus_half, subln = part(22, 2), part(24, 1)
    subln_scaled, neg_lam, lam_sum, lam_exp = part(25, 1), part(26, 1), part(28, 2), part(30, 2)
    mean_var, inv_std, var_eps = part(32, 4), part(36, 2), part(38, 2)
    eps_sum = part(42, 2)
    stats = part(48, TT * CHUNKS * 6)
    lam_in = at("lam_in", [P, 4, HALF_DIM], F32, A0 + 23 * KB)
    lam_prod = at("lam_prod", [P, 2, HALF_DIM], F32, H0 + 64 * KB)

    spill = nc.dram_tensor("ln1_spill", [P, TT, D_MODEL], F32).ap()

    def bank(name, first, count):
        return nc.alloc_psum_tensor(name, [P, count, NC], F32)

    proj_ps = [bank("proj_even", 0, TT), bank("proj_odd", 2, TT)]
    acc_ps = proj_ps[0]
    scores_ps = bank("scores_ps", 4, 2)
    turn_ps = bank("turn_ps", 6, 1)
    out_ps = bank("out_ps", 7, 1)
    big_turn = [proj_ps[1], scores_ps]
    piece_ps = [scores_ps[:, 0, :], scores_ps[:, 1, :], turn_ps[:, 0, :], out_ps[:, 0, :]]

    sems = {}

    def sem(name):
        sems[name] = nc.alloc_semaphore(name)
        return sems[name]

    w_loaded = [sem(f"w_loaded{s}") for s in range(SLOTS)]
    side_loaded = [sem(f"side_loaded{s}") for s in range(SLOTS)]
    side_rounded, side_split = sem("side_rounded"), sem("side_split")
    w_rounded, w_split, w_used = sem("w_rounded"), sem("w_split"), sem("w_used")
    ident_loaded, tables_loaded = sem("ident_loaded"), sem("tables_loaded")
    x_loaded = [sem(f"x_loaded{c}") for c in range(CHUNKS)]
    lam_loaded, gb1_loaded, gb2_loaded = sem("lam_loaded"), sem("gb1_loaded"), sem("gb2_loaded")
    lam_mult, lam_summed, lam_exped, lam_ready = (
        sem("lam_mult"), sem("lam_summed"), sem("lam_exped"), sem("lam_ready"))
    powers_ready = sem("powers_ready")
    turned, turn_rounded, turn_split = sem("turned"), sem("turn_rounded"), sem("turn_split")
    proj_done, v_copied = sem("proj_done"), sem("v_copied")
    rope_terms, roped = sem("rope_terms"), sem("roped")
    qk_turned, qkT_copied = sem("qk_turned"), sem("qkT_copied")
    scores_done, masked, max_found = sem("scores_done"), sem("masked"), sem("max_found")
    exp_done, sum_inverted = sem("exp_done"), sem("sum_inverted")
    diff_scaled, combined = sem("diff_scaled"), sem("combined")
    probs_turned, probsT_copied = sem("probs_turned"), sem("probsT_copied")
    pv_done, squared = sem("pv_done"), sem("squared")
    mean_ready, root_ready, scale_ready = sem("mean_ready"), sem("root_ready"), sem("scale_ready")
    o_ready, o_turned = sem("o_ready"), sem("o_turned")
    mix_rounded, mix_split = sem("mix_rounded"), sem("mix_split")
    out_done, y1_summed, y1_stats = sem("out_done"), sem("y1_summed"), sem("y1_stats")
    moments, var_ready, std_ready = sem("moments"), sem("var_ready"), sem("std_ready")
    centred, x1_ready, spilled = sem("centred"), sem("x1_ready"), sem("spilled")
    ff1_done, relu_done, hid_squared = sem("ff1_done"), sem("relu_done"), sem("hid_squared")
    hid_turned, hid_rounded, hid_split = sem("hid_turned"), sem("hid_rounded"), sem("hid_split")
    x1_back = sem("x1_back")
    ff2_done, y2_summed, y2_stats = sem("ff2_done"), sem("y2_summed"), sem("y2_stats")
    y2_ready, stored = sem("y2_ready"), sem("stored")

    x_d = x.rearrange("b (t p) d -> p (b t) d", p=P)
    out_d = out.rearrange("b (t p) d -> p (b t) d", p=P)
    w_in_d = w_in.rearrange("l (u k p) (g s h d) -> p (l u) k g s h d", k=KU, p=P, g=2, s=3, d=HEAD_DIM)

    def by_unit(w):
        return w.rearrange("l (u k p) (c n) -> p (l u) k c n", k=KU, p=P, n=NC)

    w_out_d, w_ff1_d, w_ff2_d = by_unit(w_out), by_unit(w_ff1), by_unit(w_ff2)

    def one(i):
        return bass.ds(i, 1)

    HC = 3 * HEAD_DIM

    def load_head_unit(sp, kind, h, head, k, first_lap=False):
        slot = k % SLOTS
        if not first_lap:
            sp.wait_ge(w_split, UPH * h + k - (SLOTS - 1))
        dst = w_raw[:, slot, 0:KU * HC].rearrange("p (k s d) -> p k s d", k=KU, s=3)
        for kk in range(KU):
            src = w_in_d[:, k, kk, kind, :, one(head), :].rearrange("p s h d -> p s (h d)")
            sp.dma_start(dst[:, kk], src).then_inc(w_loaded[slot], 16)

    def load_chunk_unit(sp, w, u, row, chunk, slot, back=SLOTS):
        sp.wait_ge(w_split, u - (back - 1))
        dst = w_raw[:, slot, :].rearrange("p (k n) -> p k n", k=KU)
        src = w[:, row, :, chunk, :] if isinstance(chunk, int) else (
            w[:, row, :, one(chunk), :].rearrange("p k c n -> p k (c n)"))
        sp.dma_start(dst, src).then_inc(w_loaded[slot], 16)

    def sync_program(sp):
        for k in range(UPH):
            if k < CHUNKS:
                cols = slice(k * NC, (k + 1) * NC)
                sp.dma_start(y1[:, :, cols], x_d[:, :, cols]).then_inc(x_loaded[k], 16)
            load_head_unit(sp, 0, 0, 0, k, first_lap=k < SLOTS)
        for kind in range(2):
            first = 1 if kind == 0 else 0
            with sp.Fori(first, N_DIFF) as j:
                for k in range(UPH):
                    load_head_unit(sp, kind, j + N_DIFF * kind, j, k)
        with sp.Fori(0, CHUNKS - 1) as n:
            for k in range(UPH):
                load_chunk_unit(sp, w_out_d, UPH * n + (U_OUT + k), k, n, k % SLOTS)
        sp.wait_ge(w_used, U_OUT + UPH)
        for k in range(SLOTS):
            sp.dma_start(side_raw[:, k, :].rearrange("p (k n) -> p k n", k=KU),
                         w_ff1_d[:, k, :, 0, :]).then_inc(side_loaded[k], 16)
        for k in range(UPH):
            load_chunk_unit(sp, w_out_d, U_OUT + UPH * (CHUNKS - 1) + k, k, CHUNKS - 1, k % SLOTS)
        for k in range(SLOTS, UPH):
            load_chunk_unit(sp, w_ff1_d, U_FF1 + k, k, 0, k % SLOTS, back=2 * SLOTS)
        with sp.Fori(1, CHUNKS_FF) as n:
            for k in range(UPH):
                load_chunk_unit(sp, w_ff1_d, UPH * n + (U_FF1 + k), k, n, k % SLOTS)
        with sp.Fori(0, CHUNKS - 1) as n:
            with sp.Fori(0, UPF // SLOTS) as lap:
                for k in range(SLOTS):
                    load_ff2_unit(sp, UPF * n + SLOTS * lap + (U_FF2 + k), SLOTS * lap + k, n, k)
        for k in range(UPF):
            load_ff2_unit(sp, U_FF2 + UPF * (CHUNKS - 1) + k, k, CHUNKS - 1, k % SLOTS)
            if k == UPF * 3 // 4:
                sp.wait_ge(w_used, U_FF2 + UPF * (CHUNKS - 1) + UPF // 2)
                for n, v in enumerate((ln2_g, ln2_b)):
                    sp.dma_start(ln2_gb[:, n, :], v.partition_broadcast(P).rearrange(
                        "p l d -> p (l d)")).then_inc(gb2_loaded, 16)
        for i, (tt, cols) in enumerate(LAST_PIECES):
            sp.wait_ge(y2_ready, i + 1)
            sp.dma_start(out_d[:, tt, cols], y2[:, tt, cols]).then_inc(stored, 16)
        sp.wait_ge(stored, 16 * len(LAST_PIECES))

    def load_ff2_unit(sp, u, row, chunk, slot):
        sp.wait_ge(w_split, u - (SLOTS - 1))
        dst = w_raw[:, slot, :].rearrange("p (k n) -> p k n", k=KU)
        if isinstance(row, int):
            src = w_ff2_d[:, row, :, chunk, :]
        else:
            src = w_ff2_d[:, one(row), :, one(chunk), :].rearrange("p u k c n -> p (u k) (c n)")
        sp.dma_start(dst, src).then_inc(w_loaded[slot], 16)

    def tensor_program(pe):
        def transpose_chunk(c):
            pe.wait_ge(x_loaded[c], 16)
            dst = big_turn[c % 2].rearrange("p b n -> p (b n)")
            for t in range(TPC):
                for tt in range(TT):
                    k = c * TPC + t
                    ins = pe.transpose(dst[:, t * SEQ + tt * P:t * SEQ + (tt + 1) * P],
                                       y1[:, tt, k * P:(k + 1) * P], ident_t[:, :])
            ins.then_inc(turned, 1)

        def transpose_piece(i):
            tt, c = PIECES[i]
            pe.wait_ge(x1_ready, i + 1)
            if i >= 4:
                pe.wait_ge(turn_split, CHUNKS + i - 3)
            for t in range(TPC):
                k = c * TPC + t
                ins = pe.transpose(piece_ps[i % 4][:, t * P:(t + 1) * P],
                                   y1[:, tt, k * P:(k + 1) * P], ident_t[:, :])
            ins.then_inc(turned, 1)

        def half_products(k, slot, left_hi, left_lo, acc, cols, kts, tt, right):
            right_hi, right_lo = right
            toks = slice(tt * P, (tt + 1) * P)
            for kk in range(KU):
                t = KU * k + kk
                hi, lo = left_hi(t), left_lo(t)
                w = slice(kk * cols, (kk + 1) * cols)
                pe.matmul(acc[:, tt, 0:cols], hi[:, toks], right_hi[:, slot, w],
                          start=(t == 0), stop=False)
                pe.matmul(acc[:, tt, 0:cols], hi[:, toks], right_lo[:, slot, w],
                          start=False, stop=False)
                ins = pe.matmul(acc[:, tt, 0:cols], lo[:, toks], right_hi[:, slot, w],
                                start=False, stop=(t == kts - 1))
            return ins

        def products(u, k, left_hi, left_lo, acc, cols, kts, free=None, tok_done=None, tts=(0, 1),
                     between=None, side=False):
            if side:
                pe.wait_ge(side_split, k + 1)
            else:
                pe.wait_ge(w_split, u + 1)
            for tt in tts:
                if free is not None and k == 0:
                    free(tt)
                ins = half_products(k, k % SLOTS, left_hi, left_lo, acc, cols, kts, tt,
                                    (side_hi, side_lo) if side else (w_hi, w_lo))
                if tt == TT - 1:
                    ins.then_inc(w_used, 1)
                elif tok_done is not None and KU * (k + 1) == kts:
                    ins.then_inc(tok_done, 1)
                if tt == 0 and between is not None:
                    between()

        def tok_by_tok(unit, first, count, inside=None):
            for tt in range(TT):
                for k in range(first, first + count):
                    unit(k, tts=(tt,))
                    if inside and (tt, k) in inside:
                        inside[tt, k]()

        def turn_qk(h):
            pe.wait_ge(roped, h + 1)
            for s in range(2):
                for tt in range(TT):
                    ins = pe.transpose(turn_ps[:, 0, s * SEQ + tt * P:s * SEQ + (tt + 1) * P],
                                       qk[:, tt, s * P:(s + 1) * P], ident_t[:, :])
            ins.then_inc(qk_turned, 1)

        def score(h, maps):
            pe.wait_ge(qkT_copied, h + 1)
            width = P // maps
            for m in range(maps):
                rows = slice(m * width, (m + 1) * width)
                for tt in range(TT):
                    ins = pe.matmul(scores_ps[:, m, keys_of(tt)], qkT[rows, 0, tt * P:(tt + 1) * P],
                                    qkT[rows, 1, 0:(tt + 1) * P], start=True, stop=True)
            ins.then_inc(scores_done, 1)

        def turn_probs(h, maps):
            if maps == 2:
                pe.wait_ge(combined, h + 1)
            else:
                pe.wait_ge(exp_done, h + 1)
            if not (isinstance(h, int) and h == 0):
                pe.wait_ge(mix_split, h)
            source = diff_probs if maps == 2 else probs[:, 0, :]
            for b in range(3):
                ins = pe.transpose(out_ps[:, 0, b * P:(b + 1) * P], source[:, b * P:(b + 1) * P],
                                   ident_t[:, :])
            ins.then_inc(probs_turned, 1)

        def weigh_values(h):
            pe.wait_ge(probsT_copied, h + 1)
            pe.matmul(out_ps[:, 0, 0:P], probsT[:, 0:P], v_sb[:, 0, :], start=True, stop=True)
            pe.matmul(out_ps[:, 0, P:2 * P], probsT[:, P:2 * P], v_sb[:, 0, :], start=True, stop=False)
            pe.matmul(out_ps[:, 0, P:2 * P], probsT[:, 2 * P:3 * P], v_sb[:, 1, :],
                      start=False, stop=True).then_inc(pv_done, 1)

        def turn_output(h):
            pe.wait_ge(o_ready, h + 1)
            for tt in range(TT):
                ins = pe.transpose(out_ps[:, 0, SEQ + tt * P:SEQ + (tt + 1) * P], o_sb[:, tt, :],
                                   ident_t[:, :])
            ins.then_inc(o_turned, 1)

        def slot(h, parity, att_maps, has_out, unit):
            for k in range(UPH):
                unit(k)
                if k == 0 and has_out:
                    turn_output(h - 2)
                if k == 1 and att_maps:
                    turn_qk(h - 1)
                if k == 2 and att_maps:
                    score(h - 1, att_maps)
                if k == 5 and att_maps:
                    turn_probs(h - 1, att_maps)
                if k == 6 and att_maps:
                    weigh_values(h - 1)

        def head_slot(h, parity, att_maps, has_out):
            acc = proj_ps[parity]

            def unit(k):
                if k == 0 and not (isinstance(h, int) and h < 2):
                    pe.wait_ge(roped, h - 1)
                if isinstance(h, int) and h == 0:
                    for c in {0: (0, 1), 1: (2,), 2: (3,)}.get(k, ()):
                        if c >= 2:
                            pe.wait_ge(turn_split, c - 1)
                        transpose_chunk(c)
                    pe.wait_ge(turn_split, k * KU // TPC + 1)
                products(UPH * h + k, k, lambda i: xT_hi[:, i, :], lambda i: xT_lo[:, i, :], acc, HC,
                         KT)

            slot(h, parity, att_maps, has_out, unit)
        pe.wait_ge(ident_loaded, 16)
        head_slot(0, 0, 0, False)
        head_slot(1, 1, 2, False)
        with pe.Fori(1, N_DIFF // 2) as j:
            head_slot(2 * j, 0, 2, True)
            head_slot(2 * j + 1, 1, 2, True)
        head_slot(N_DIFF, 0, 2, True)
        head_slot(N_DIFF + 1, 1, 1, True)
        with pe.Fori(N_DIFF // 2 + 1, HEADS // 2) as j:
            head_slot(2 * j, 0, 1, True)
            head_slot(2 * j + 1, 1, 1, True)

        def out_unit(n, k, tts=(0, 1), between=None):
            def free(tt):
                if isinstance(n, int) and n == 0:
                    pe.wait_ge(roped, HEADS - 1)
                else:
                    pe.wait_ge(y1_summed, TT * n - TT + tt + 1)
            products(UPH * n + (U_OUT + k), k, lambda i: mixT_hi[:, i, :],
                     lambda i: mixT_lo[:, i, :], acc_ps, NC, KT, free, out_done, tts, between)

        for k in range(UPH):
            if k == UPH - 1:
                pe.wait_ge(mix_split, HEADS)
            out_unit(0, k, between={2: lambda: score(HEADS - 1, 1),
                                    4: lambda: weigh_values(HEADS - 1),
                                    5: lambda: turn_output(HEADS - 1)}.get(k))
            if k == 0:
                turn_output(HEADS - 2)
            if k == 1:
                turn_qk(HEADS - 1)
            if k == 3:
                turn_probs(HEADS - 1, 1)
        with pe.Fori(1, CHUNKS - 1) as n:
            for k in range(UPH):
                out_unit(n, k)
        for k in range(UPH - SLOTS):
            out_unit(CHUNKS - 1, k)
        tok_by_tok(lambda k, tts: out_unit(CHUNKS - 1, k, tts), UPH - SLOTS, SLOTS,
                   {(1, UPH - 2): lambda: transpose_piece(0)})

        def ff1_unit(i, k, tts=(0, 1), side=False):
            def free(tt):
                if isinstance(i, int) and i == 0:
                    pe.wait_ge(y1_summed, TT * CHUNKS - TT + tt + 1)
                else:
                    pe.wait_ge(relu_done, TT * i - TT + tt + 1)
            products(UPH * i + (U_FF1 + k), k, lambda t: x1T_hi[:, t, :],
                     lambda t: x1T_lo[:, t, :], acc_ps, NC, KT, free, ff1_done, tts,
                     side=side)

        def first_ff1_unit(k, tts=(0, 1)):
            for tt in tts:
                pe.wait_ge(turn_split, CHUNKS + PIECES.index((tt, KU * k // TPC)) + 1)
            ff1_unit(0, k, tts, side=k < SLOTS)

        def turn_hidden(i):
            pe.wait_ge(hid_squared, i + 1)
            dst = scores_ps.rearrange("p b n -> p (b n)")
            for t in range(TPC):
                for tt in range(TT):
                    ins = pe.transpose(dst[:, t * SEQ + tt * P:t * SEQ + (tt + 1) * P],
                                       relu[:, tt, t * P:(t + 1) * P], ident_t[:, :])
            ins.then_inc(hid_turned, 1)

        after = {(0, 0): 1, (0, 2): 2, (0, 4): 3, (0, 6): 4, (1, 0): 5, (1, 2): 6, (1, 3): 7}
        tok_by_tok(first_ff1_unit, 0, UPH,
                   {at: lambda i=i: transpose_piece(i) for at, i in after.items()})
        with pe.Fori(1, CHUNKS_FF) as i:
            for k in range(UPH):
                ff1_unit(i, k)
                if k == 1:
                    turn_hidden(i - 1)

        def hid(early, late):
            return lambda t: early[:, t, :] if t < EARLY else late[:, t - EARLY, :]

        def ff2_unit(n, k, tts=(0, 1)):
            def free(tt):
                if isinstance(n, int) and n == 0:
                    pe.wait_ge(relu_done, TT * CHUNKS_FF - TT + tt + 1)
                else:
                    pe.wait_ge(y2_summed, TT * n - TT + tt + 1)
            products(UPF * n + (U_FF2 + k), k, hid(hidT_hi, late_hi), hid(hidT_lo, late_lo), acc_ps,
                     NC, KT_FF, free, ff2_done, tts)

        for k in range(UPF):
            if KU * k == EARLY:
                pe.wait_ge(hid_split, CHUNKS_FF)
            ff2_unit(0, k)
            if k == 1:
                turn_hidden(CHUNKS_FF - 1)
        with pe.Fori(1, CHUNKS - 1) as n:
            for k in range(UPF):
                ff2_unit(n, k)
        for k in range(UPF - SLOTS):
            ff2_unit(CHUNKS - 1, k)
        tok_by_tok(lambda k, tts: ff2_unit(CHUNKS - 1, k, tts), UPF - SLOTS, SLOTS)

    def scalar_program(act):
        def round_unit(u, slot, lap, cols, fresh=False, back=SLOTS, units=1):
            if cols == KU * HC:
                loads = KU * lap
            else:
                loads = lap + (KU - 1) * (U_OUT // SLOTS)
            act.wait_ge(w_loaded[slot], 16 * loads)
            if not fresh:
                act.wait_ge(w_used, u - (back - 1))
            act.activation(w_hi[:, slot, 0:cols], w_raw[:, slot, 0:cols], ACT.Copy).then_inc(
                w_rounded, units)

        def ahead(first, k, cols=KU * NC):
            round_unit(first + (k + SLOTS), k % SLOTS, first // SLOTS + (k // SLOTS + 2), cols)

        def ahead_mlp(first, k, back=SLOTS, units=1):
            round_unit(first + (k + SLOTS), k % SLOTS, first // SLOTS + (k // SLOTS + 1), KU * NC,
                       back=back, units=units)

        def round_turned(c, hi):
            act.wait_ge(turned, c + 1)
            src = big_turn[c % 2].rearrange("p b n -> p (b n)")
            act.activation(hi.rearrange("p k t -> p (k t)"), src, ACT.Copy).then_inc(turn_rounded, 1)

        def copy_v(h, parity):
            act.wait_ge(w_used, UPH * h + UPH)
            act.activation(v_sb[:, :, :], proj_ps[parity][:, :, 2 * P:3 * P], ACT.Copy).then_inc(
                v_copied, 1)

        def copy_qkT(h):
            act.wait_ge(qk_turned, h + 1)
            act.activation(qkT[:, :, :].rearrange("p s t -> p (s t)"), turn_ps[:, 0, :],
                           ACT.Copy).then_inc(qkT_copied, 1)

        def exponentials(h, maps):
            act.wait_ge(max_found, 2 * h + 2)
            for tt in range(TT):
                for m in range(maps):
                    i = 2 * tt + m
                    ins = act.activation(probs[:, m, keys_of(tt)], scores[:, m, keys_of(tt)], ACT.Exp,
                                         bias=neg_max[:, i:i + 1], accum_out=row_sum[:, i:i + 1])
            ins.then_inc(exp_done, 1)

        def copy_probsT(h):
            act.wait_ge(probs_turned, h + 1)
            act.activation(probsT[:, :], out_ps[:, 0, 0:KEYS], ACT.Copy).then_inc(probsT_copied, 1)

        def square_sums(h):
            act.wait_ge(pv_done, h + 1)
            act.wait_ge(sum_inverted, h + 1)
            for tt in range(TT):
                ins = act.activation(squares[:, tt, :], out_ps[:, 0, tt * P:(tt + 1) * P], ACT.Square,
                                     scale=inv_sum[:, 2 * tt:2 * tt + 1],
                                     accum_out=sum_sq[:, tt:tt + 1])
            ins.then_inc(squared, 1)

        def scale_output(h, maps):
            if maps == 2:
                act.wait_ge(scale_ready, h + 1)
            else:
                act.wait_ge(pv_done, h + 1)
                act.wait_ge(sum_inverted, h + 1)
            for tt in range(TT):
                by = o_scale[:, tt:tt + 1] if maps == 2 else inv_sum[:, 2 * tt:2 * tt + 1]
                ins = act.activation(o_sb[:, tt, :], out_ps[:, 0, tt * P:(tt + 1) * P], ACT.Copy,
                                     scale=by)
            ins.then_inc(o_ready, 1)

        def round_mix(h, maps):
            act.wait_ge(o_turned, h + 1)
            dst = mixT_hi[:, h, :] if isinstance(h, int) else (
                mixT_hi[:, one(h), :].rearrange("p h t -> p (h t)"))
            act.activation(dst, out_ps[:, 0, SEQ:2 * SEQ], ACT.Copy,
                           scale=subln_scaled if maps == 2 else 1.0).then_inc(mix_rounded, 1)

        def slot(h, parity, att_maps, out_maps, columns=None):
            cols = columns or KU * HC
            first = UPH * h
            if att_maps:
                copy_v(h - 1, 1 - parity)
            ahead(first, 0, cols)
            if out_maps:
                round_mix(h - 2, out_maps)
            ahead(first, 1, cols)
            if att_maps:
                copy_qkT(h - 1)
            ahead(first, 2, cols)
            if att_maps:
                exponentials(h - 1, att_maps)
            ahead(first, 3, cols)
            cols = KU * NC if isinstance(h, int) and h == HEADS - 1 else cols
            ahead(first, 4, cols)
            ahead(first, 5, cols)
            if att_maps:
                copy_probsT(h - 1)
            ahead(first, 6, cols)
            if att_maps == 2:
                square_sums(h - 1)
            ahead(first, 7, cols)
            if att_maps:
                scale_output(h - 1, att_maps)

        for c in range(SLOTS):
            round_unit(c, c, 1, KU * HC, fresh=True)
            round_turned(c, xT_hi[:, c * TPC:(c + 1) * TPC, :])
        for k in range(SLOTS):
            ahead(0, k, KU * HC)
        act.wait_ge(lam_loaded, 16 * 5)
        act.activation(subln_scaled, subln, ACT.Copy, scale=(1.0 - LAMBDA_INIT) * HEAD_DIM ** 0.5)
        act.wait_ge(lam_summed, 2)
        act.activation(lam_exp, lam_sum, ACT.Exp).then_inc(lam_exped, 1)
        for k in range(SLOTS, UPH):
            ahead(0, k, KU * HC)
        slot(1, 1, 2, 0)
        with act.Fori(1, N_DIFF // 2) as j:
            slot(2 * j, 0, 2, 2)
            slot(2 * j + 1, 1, 2, 2)
        slot(N_DIFF, 0, 2, 2)
        slot(N_DIFF + 1, 1, 1, 2)
        with act.Fori(N_DIFF // 2 + 1, HEADS // 2 - 1) as j:
            slot(2 * j, 0, 1, 1)
            slot(2 * j + 1, 1, 1, 1)
        slot(HEADS - 2, 0, 1, 1)
        slot(HEADS - 1, 1, 1, 1)

        copy_v(HEADS - 1, 1)
        round_mix(HEADS - 2, 1)
        ahead(U_OUT, 0)
        ahead(U_OUT, 1)
        copy_qkT(HEADS - 1)
        exponentials(HEADS - 1, 1)
        ahead(U_OUT, 2)
        ahead(U_OUT, 3)
        copy_probsT(HEADS - 1)
        scale_output(HEADS - 1, 1)
        ahead(U_OUT, 4)
        round_mix(HEADS - 1, 1)
        ahead(U_OUT, 5)
        ahead(U_OUT, 6)
        ahead(U_OUT, 7)
        with act.Fori(1, CHUNKS - 1) as n:
            for k in range(UPH):
                ahead(UPH * n + U_OUT, k)

        def round_piece(i):
            tt, c = PIECES[i]
            act.wait_ge(turned, CHUNKS + i + 1)
            act.activation(x1T_hi[:, c * TPC:(c + 1) * TPC, tt * P:(tt + 1) * P],
                           piece_ps[i % 4].rearrange("p (k t) -> p k t", k=TPC),
                           ACT.Copy).then_inc(turn_rounded, 1)

        last_out = U_OUT + UPH * (CHUNKS - 1)
        for k in range(SLOTS):
            ahead(last_out, k)
            act.wait_ge(side_loaded[k], 16)
            act.activation(side_hi[:, k, :], side_raw[:, k, :], ACT.Copy).then_inc(side_rounded, 1)
        for k in range(SLOTS):
            round_piece(k)
            ahead_mlp(U_FF1, k, back=2 * SLOTS, units=SLOTS + 1 if k == 0 else 1)
        for i in range(SLOTS, len(PIECES)):
            round_piece(i)

        def relu_chunk(i):
            for tt in range(TT):
                if tt == 0:
                    act.wait_ge(ff1_done, i + 1)
                else:
                    act.wait_ge(w_used, UPH * i + (U_FF1 + UPH))
                if not (isinstance(i, int) and i == 0):
                    act.wait_ge(hid_turned, i)
                act.activation(relu[:, tt, :], acc_ps[:, tt, :], ACT.Relu).then_inc(relu_done, 1)

        def round_hidden(i, last=False):
            act.wait_ge(hid_turned, i + 1)
            dst = late_hi if last else hidT_hi[:, bass.ds(i * TPC, TPC), :]
            act.activation(dst.rearrange("p k t -> p (k t)"),
                           scores_ps.rearrange("p b n -> p (b n)"), ACT.Copy).then_inc(hid_rounded, 1)

        def ff1_slot(i, first, begin=0):
            for k in range(begin, UPH):
                if k == 2 and not (isinstance(i, int) and i == 0):
                    round_hidden(i - 1)
                if k == UPH - 1:
                    relu_chunk(i)
                ahead_mlp(first, k)

        ff1_slot(0, U_FF1, begin=SLOTS)
        with act.Fori(1, CHUNKS_FF) as i:
            ff1_slot(i, UPH * i + U_FF1)

        for k in range(SLOTS):
            if k == 2:
                round_hidden(CHUNKS_FF - 1, last=True)
            ahead_mlp(U_FF2, k)
        with act.Fori(1, (U_END - U_FF2) // SLOTS - 1) as lap:
            for k in range(SLOTS):
                ahead_mlp(SLOTS * lap + U_FF2, k)

    def vector_program(dve):
        def split_unit(u, slot, cols, units=1):
            dve.wait_ge(w_rounded, u + 1)
            dve.tensor_tensor(w_lo[:, slot, 0:cols], w_raw[:, slot, 0:cols],
                              w_hi[:, slot, 0:cols].bitcast(F32),
                              ALU.subtract).then_inc(w_split, units)

        def ahead(first, k, cols=KU * NC, units=1):
            split_unit(first + (k + SLOTS), k % SLOTS, cols, units)

        def split_turned(c, hi, lo):
            dve.wait_ge(turn_rounded, c + 1)
            src = big_turn[c % 2].rearrange("p b n -> p (b n)")
            dve.tensor_tensor(lo.rearrange("p k t -> p (k t)"), src,
                              hi.rearrange("p k t -> p (k t)").bitcast(F32),
                              ALU.subtract).then_inc(turn_split, 1)

        def rope(h, parity, maps):
            width = P // maps
            half = width // 2
            groups = 2 * maps
            t0 = (T_ROPE_A if maps == 2 else T_ROPE_B) - P
            tabs = tables[:, t0:t0 + 2 * TT * width].rearrange("p (c t d) -> p c t d", c=2, t=TT)

            def grouped(ap):
                return ap.rearrange("p t (g d) -> p t g d", g=groups)

            def spread(ap):
                return ap.unsqueeze(2).to_broadcast([P, TT, groups, ap.shape[-1]])

            src = grouped(proj_ps[parity][:, :, 0:2 * P])
            sin = tabs[:, 1]
            dve.wait_ge(v_copied, h + 1)
            dve.tensor_tensor(grouped(rope_cos[:, :, :]), src, spread(tabs[:, 0]),
                              ALU.mult).then_inc(rope_terms, 1)
            dve.tensor_tensor(grouped(rope_sin[:, :, :])[:, :, :, 0:half], src[:, :, :, half:width],
                              spread(sin[:, :, 0:half]), ALU.mult).then_inc(rope_terms, 1)
            dve.tensor_tensor(grouped(rope_sin[:, :, :])[:, :, :, half:width], src[:, :, :, 0:half],
                              spread(sin[:, :, half:width]), ALU.mult).then_inc(rope_terms, 1)
            dve.wait_ge(rope_terms, 3 * h + 3)
            dve.tensor_tensor(qk[:, :, :], rope_cos[:, :, :], rope_sin[:, :, :],
                              ALU.add).then_inc(roped, 1)

        def mask_and_max(h, maps):
            t0 = (T_MASK_A if maps == 2 else T_MASK_B) - P
            mask = tables[:, t0:t0 + KEYS].unsqueeze(1).to_broadcast([P, maps, KEYS])
            scale = float((P // maps) ** -0.5)
            dve.wait_ge(scores_done, h + 1)
            dve.scalar_tensor_tensor(out=scores[:, 0:maps, :], in0=scores_ps[:, 0:maps, 0:KEYS],
                                     scalar=scale, in1=mask, op0=ALU.mult,
                                     op1=ALU.add).then_inc(masked, 1)
            dve.wait_ge(masked, h + 1)
            for tt in range(TT):
                dve.tensor_reduce(neg_max[:, 2 * tt:2 * tt + maps], scores[:, 0:maps, keys_of(tt)],
                                  AX.X, ALU.max, negate=True).then_inc(max_found, 1)

        def invert_sums(h, maps):
            dve.wait_ge(exp_done, h + 1)
            if maps == 2:
                dve.reciprocal(inv_sum[:, :], row_sum[:, :]).then_inc(sum_inverted, 1)
            else:
                dve.reciprocal(inv_sum[:, 0:4:2], row_sum[:, 0:4:2]).then_inc(sum_inverted, 1)

        def combine(h):
            dve.wait_ge(sum_inverted, h + 1)
            dve.scalar_tensor_tensor(out=diff_scale, in0=row_sum[:, 0:4:2], scalar=neg_lam,
                                     in1=inv_sum[:, 1:4:2], op0=ALU.mult,
                                     op1=ALU.mult).then_inc(diff_scaled, 1)
            dve.wait_ge(diff_scaled, h + 1)
            for tt in range(TT):
                ins = dve.scalar_tensor_tensor(
                    out=diff_probs[:, keys_of(tt)], in0=probs[:, 1, keys_of(tt)],
                    scalar=diff_scale[:, tt:tt + 1], in1=probs[:, 0, keys_of(tt)],
                    op0=ALU.mult, op1=ALU.add)
            ins.then_inc(combined, 1)

        def split_mix(h, maps):
            dve.wait_ge(mix_rounded, h + 1)

            def row(t):
                return t[:, h, :] if isinstance(h, int) else (
                    t[:, one(h), :].rearrange("p h t -> p (h t)"))
            src, hi, lo = out_ps[:, 0, SEQ:2 * SEQ], row(mixT_hi).bitcast(F32), row(mixT_lo)
            if maps == 2:
                dve.scalar_tensor_tensor(out=lo, in0=src, scalar=subln_scaled, in1=hi, op0=ALU.mult,
                                         op1=ALU.subtract).then_inc(mix_split, 1)
            else:
                dve.tensor_tensor(lo, src, hi, ALU.subtract).then_inc(mix_split, 1)

        def slot(h, parity, rope_maps, att_maps, out_maps):
            cols = KU * HC
            first = UPH * h
            if rope_maps:
                rope(h - 1, 1 - parity, rope_maps)
            ahead(first, 0, cols)
            if out_maps:
                split_mix(h - 2, out_maps)
            ahead(first, 1, cols)
            if att_maps:
                mask_and_max(h - 1, att_maps)
            ahead(first, 2, cols)
            if att_maps:
                invert_sums(h - 1, att_maps)
            if att_maps == 2:
                combine(h - 1)
            ahead(first, 3, cols)
            cols = KU * NC if isinstance(h, int) and h == HEADS - 1 else cols
            ahead(first, 4, cols)
            ahead(first, 5, cols)
            ahead(first, 6, cols)
            ahead(first, 7, cols)

        dve.memset(minus_half, -0.5).then_inc(powers_ready, 1)
        dve.memset(eps_sum, HEAD_DIM * EPS).then_inc(powers_ready, 1)
        for c in range(SLOTS):
            split_unit(c, c, KU * HC)
            split_turned(c, xT_hi[:, c * TPC:(c + 1) * TPC, :], xT_lo[:, c * TPC:(c + 1) * TPC, :])
        for k in range(SLOTS):
            ahead(0, k, KU * HC)
        dve.wait_ge(lam_loaded, 16 * 5)
        for n in range(2):
            dve.tensor_tensor(lam_prod[:, n, :], lam_in[:, 2 * n, :], lam_in[:, 2 * n + 1, :],
                              ALU.mult).then_inc(lam_mult, 1)
        dve.wait_ge(lam_mult, 2)
        for n in range(2):
            dve.reduce_sum(lam_sum[:, n:n + 1], lam_prod[:, n, :], AX.X).then_inc(lam_summed, 1)
        for k in range(SLOTS, UPH):
            ahead(0, k, KU * HC)
        dve.wait_ge(lam_exped, 1)
        dve.scalar_tensor_tensor(out=neg_lam, in0=lam_exp[:, 1:2], scalar=LAMBDA_INIT,
                                 in1=lam_exp[:, 0:1], op0=ALU.subtract,
                                 op1=ALU.subtract).then_inc(lam_ready, 1)
        dve.wait_ge(lam_ready, 1)
        dve.wait_ge(tables_loaded, 16)
        slot(1, 1, 2, 2, 0)
        with dve.Fori(1, N_DIFF // 2) as j:
            slot(2 * j, 0, 2, 2, 2)
            slot(2 * j + 1, 1, 2, 2, 2)
        slot(N_DIFF, 0, 2, 2, 2)
        slot(N_DIFF + 1, 1, 1, 1, 2)
        with dve.Fori(N_DIFF // 2 + 1, HEADS // 2 - 1) as j:
            slot(2 * j, 0, 1, 1, 1)
            slot(2 * j + 1, 1, 1, 1, 1)
        slot(HEADS - 2, 0, 1, 1, 1)
        slot(HEADS - 1, 1, 1, 1, 1)

        def add_residual(n, y, tok_done, end, summed, tts=(0, 1)):
            for tt in tts:
                if tt == 0:
                    dve.wait_ge(tok_done, n + 1)
                else:
                    dve.wait_ge(w_used, end)
                cols = slice(n * NC, (n + 1) * NC) if isinstance(n, int) else bass.ds(n * NC, NC)
                dve.scalar_tensor_tensor(out=y[:, tt, cols], in0=y[:, tt, cols], scalar=ALPHA,
                                         in1=acc_ps[:, tt, :], op0=ALU.mult,
                                         op1=ALU.add).then_inc(summed, 1)

        def tok_stats(n, tt, y, summed, stat_done):
            dve.wait_ge(summed, TT * n + tt + 1)
            cols = slice(n * NC, (n + 1) * NC) if isinstance(n, int) else bass.ds(n * NC, NC)
            first = tt * CHUNKS * 6 + n * 6
            where = slice(first, first + 6) if isinstance(n, int) else bass.ds(first, 6)
            dve.bn_stats(stats[:, where], y[:, tt, cols]).then_inc(stat_done, 1)

        def tok_moments(tt, stat_done):
            dve.wait_ge(stat_done, TT * (CHUNKS - 1) + tt + 1)
            dve.bn_aggr(mean_var[:, 2 * tt:2 * tt + 2],
                        stats[:, tt * CHUNKS * 6:(tt + 1) * CHUNKS * 6]).then_inc(moments, 1)

        def centre(norm, tt, cols, y, gb):
            dve.wait_ge(moments, TT * norm + tt + 1)
            dve.scalar_tensor_tensor(out=y[:, tt, cols], in0=y[:, tt, cols],
                                     scalar=mean_var[:, 2 * tt:2 * tt + 1], in1=gb[:, 0, cols],
                                     op0=ALU.subtract, op1=ALU.mult).then_inc(centred, 1)

        def finish_norm(norm, count, tt, cols, y, gb, ready):
            dve.wait_ge(centred, count)
            dve.wait_ge(std_ready, TT * norm + tt + 1)
            dve.scalar_tensor_tensor(out=y[:, tt, cols], in0=y[:, tt, cols],
                                     scalar=inv_std[:, tt:tt + 1], in1=gb[:, 1, cols],
                                     op0=ALU.mult, op1=ALU.add).then_inc(ready, 1)

        rope(HEADS - 1, 1, 1)
        split_mix(HEADS - 2, 1)
        ahead(U_OUT, 0)
        mask_and_max(HEADS - 1, 1)
        ahead(U_OUT, 1)
        ahead(U_OUT, 2)
        ahead(U_OUT, 3)
        invert_sums(HEADS - 1, 1)
        ahead(U_OUT, 4)
        ahead(U_OUT, 5)
        split_mix(HEADS - 1, 1)
        add_residual(0, y1, out_done, U_OUT + UPH, y1_summed, (0,))
        ahead(U_OUT, 6)
        add_residual(0, y1, out_done, U_OUT + UPH, y1_summed, (1,))
        ahead(U_OUT, 7)
        for tt in range(TT):
            tok_stats(0, tt, y1, y1_summed, y1_stats)
        with dve.Fori(1, CHUNKS - 1) as n:
            for k in range(UPH):
                if k >= UPH - TT:
                    add_residual(n, y1, out_done, UPH * n + (U_OUT + UPH), y1_summed,
                                 (k - (UPH - TT),))
                ahead(UPH * n + U_OUT, k)
            for tt in range(TT):
                tok_stats(n, tt, y1, y1_summed, y1_stats)

        def sums_done(tt):
            add_residual(CHUNKS - 1, y1, out_done, U_FF1, y1_summed, (tt,))
            tok_stats(CHUNKS - 1, tt, y1, y1_summed, y1_stats)
            tok_moments(tt, y1_stats)

        def norm_piece(i, steps=(0, 1)):
            tt, c = PIECES[i]
            cols = slice(c * NC, (c + 1) * NC)
            if 0 in steps:
                centre(0, tt, cols, y1, ln1_gb)
            if 1 in steps:
                finish_norm(0, i + 1, tt, cols, y1, ln1_gb, x1_ready)

        def split_piece(i):
            tt, c = PIECES[i]
            dve.wait_ge(turn_rounded, CHUNKS + i + 1)
            where = (slice(None), slice(c * TPC, (c + 1) * TPC), slice(tt * P, (tt + 1) * P))
            dve.tensor_tensor(x1T_lo[where], piece_ps[i % 4].rearrange("p (k t) -> p k t", k=TPC),
                              x1T_hi[where].bitcast(F32), ALU.subtract).then_inc(turn_split, 1)

        last_out = U_OUT + UPH * (CHUNKS - 1)
        for k in range(SLOTS):
            ahead(last_out, k)
            dve.wait_ge(side_rounded, k + 1)
            dve.tensor_tensor(side_lo[:, k, :], side_raw[:, k, :], side_hi[:, k, :].bitcast(F32),
                              ALU.subtract).then_inc(side_split, 1)
        dve.wait_ge(gb1_loaded, 32)
        sums_done(0)
        norm_piece(0)
        norm_piece(1)
        split_piece(0)
        ahead(U_FF1, 0, units=SLOTS + 1)
        norm_piece(2)
        split_piece(1)
        sums_done(1)
        ahead(U_FF1, 1)
        split_piece(2)
        norm_piece(3)
        ahead(U_FF1, 2)
        split_piece(3)
        norm_piece(4)
        ahead(U_FF1, 3)
        split_piece(4)
        norm_piece(5)
        norm_piece(6)
        split_piece(5)
        norm_piece(7)
        split_piece(6)
        split_piece(7)

        def square_hidden(i):
            dve.wait_ge(relu_done, TT * i + TT)
            dve.tensor_tensor(relu[:, :, :], relu[:, :, :], relu[:, :, :], ALU.mult).then_inc(
                hid_squared, 1)

        def split_hidden(i, last=False):
            dve.wait_ge(hid_rounded, i + 1)
            hi = late_hi if last else hidT_hi[:, bass.ds(i * TPC, TPC), :]
            lo = late_lo if last else hidT_lo[:, bass.ds(i * TPC, TPC), :]
            dve.tensor_tensor(lo.rearrange("p k t -> p (k t)"),
                              scores_ps.rearrange("p b n -> p (b n)"),
                              hi.rearrange("p k t -> p (k t)").bitcast(F32),
                              ALU.subtract).then_inc(hid_split, 1)

        def ff1_slot(i, first, begin=0):
            for k in range(begin, UPH):
                if k == 2 and not (isinstance(i, int) and i == 0):
                    split_hidden(i - 1)
                ahead(first, k)
            square_hidden(i)

        ff1_slot(0, U_FF1, begin=SLOTS)
        dve.wait_ge(spilled, 16 * len(PIECES))
        with dve.Fori(1, CHUNKS_FF) as i:
            ff1_slot(i, UPH * i + U_FF1)

        def ff2_slot(n, first, units):
            with dve.Fori(0, units, SLOTS) as k0:
                for k in range(SLOTS):
                    ahead(first + k0, k)

        for n in range(CHUNKS):
            first = U_FF2 + UPF * n
            if n == 0:
                for k in range(SLOTS):
                    if k == 2:
                        split_hidden(CHUNKS_FF - 1, last=True)
                    ahead(first, k)
            last = n == CHUNKS - 1
            with dve.Fori(SLOTS if n == 0 else 0, UPF - SLOTS, SLOTS) as k0:
                for k in range(SLOTS):
                    ahead(first + k0, k)
            if not last:
                if n == 0:
                    dve.wait_ge(x1_back, 16)
                for k in range(SLOTS):
                    if k >= SLOTS - TT:
                        add_residual(n, y2, ff2_done, first + UPF, y2_summed, (k - (SLOTS - TT),))
                    ahead(first + UPF - SLOTS, k)
                for tt in range(TT):
                    tok_stats(n, tt, y2, y2_summed, y2_stats)

        dve.wait_ge(gb2_loaded, 32)
        count = len(PIECES)
        for tt in range(TT):
            add_residual(CHUNKS - 1, y2, ff2_done, U_END, y2_summed, (tt,))
            tok_stats(CHUNKS - 1, tt, y2, y2_summed, y2_stats)
            tok_moments(tt, y2_stats)
            pieces = [cols for t, cols in LAST_PIECES if t == tt]
            for cols in pieces:
                centre(1, tt, cols, y2, ln2_gb)
            for cols in pieces:
                count += 1
                finish_norm(1, count, tt, cols, y2, ln2_gb, y2_ready)

    def gpsimd_program(pool):
        pool.wait_ge(powers_ready, 2)

        def rms_scale(h):
            pool.wait_ge(squared, h + 1)
            pool.tensor_tensor(mean_sq, sum_sq, eps_sum, ALU.add).then_inc(mean_ready, 1)
            pool.wait_ge(mean_ready, h + 1)
            pool.tensor_tensor(root, mean_sq, minus_half, ALU.pow).then_inc(root_ready, 1)
            pool.wait_ge(root_ready, h + 1)
            pool.tensor_tensor(o_scale, root, inv_sum[:, 0:4:2], ALU.mult).then_inc(scale_ready, 1)

        def norm_scale(norm):
            for tt in range(TT):
                n = TT * norm + tt + 1
                pool.wait_ge(moments, n)
                pool.tensor_scalar(var_eps[:, tt:tt + 1], mean_var[:, 2 * tt + 1:2 * tt + 2], EPS,
                                   None, ALU.add).then_inc(var_ready, 1)
                pool.wait_ge(var_ready, n)
                pool.tensor_tensor(inv_std[:, tt:tt + 1], var_eps[:, tt:tt + 1],
                                   minus_half[:, tt:tt + 1], ALU.pow).then_inc(std_ready, 1)

        for n, v in enumerate((lq1, lk1, lq2, lk2)):
            pool.dma_start(lam_in[:, n, :], v.partition_broadcast(P).rearrange(
                "p l d -> p (l d)")).then_inc(lam_loaded, 16)
        pool.dma_start(subln, subln_g.rearrange("l d -> d l")).then_inc(lam_loaded, 16)
        pool.dma_start(tables[:, :], table[:, P:T_COLS]).then_inc(tables_loaded, 16)
        with pool.Fori(0, N_DIFF) as h:
            rms_scale(h)
        for n, v in enumerate((ln1_g, ln1_b)):
            pool.wait_ge(lam_summed, 2)
            pool.dma_start(ln1_gb[:, n, :], v.partition_broadcast(P).rearrange(
                "p l d -> p (l d)")).then_inc(gb1_loaded, 16)
        norm_scale(0)
        for i, (tt, c) in enumerate(PIECES):
            cols = slice(c * NC, (c + 1) * NC)
            pool.wait_ge(x1_ready, i + 1)
            pool.dma_start(spill[:, tt, cols], y1[:, tt, cols]).then_inc(spilled, 16)
        pool.wait_ge(spilled, 16 * len(PIECES))
        pool.wait_ge(w_used, U_FF2)
        pool.dma_start(y2[:, :, :], spill).then_inc(x1_back, 16)
        norm_scale(1)

    with nc.Block() as block:
        @block.sync
        def _(sp):
            sp.dma_start(ident_t[:, :], table[:, 0:P]).then_inc(ident_loaded, 16)
            sync_program(sp)

        @block.tensor
        def _(pe):
            tensor_program(pe)

        @block.scalar
        def _(act):
            scalar_program(act)

        @block.vector
        def _(dve):
            vector_program(dve)

        @block.gpsimd
        def _(pool):
            gpsimd_program(pool)


_INS = ["x", "w_in", "lambda_q1", "lambda_k1", "lambda_q2", "lambda_k2", "subln_g", "w_out",
        "ln1_g", "ln1_b", "w_ff1", "w_ff2", "ln2_g", "ln2_b"]


def kernel(**inputs):
    import concourse.bacc as bacc
    from concourse.bass_utils import run_bass_kernel_spmd

    nc = bacc.Bacc("TRN2", target_bir_lowering=False, num_devices=1)
    arrays = {f"in_{n}": np.ascontiguousarray(inputs[n]) for n in _INS}
    arrays["in_table"] = constant_table()
    args = [nc.dram_tensor(n, a.shape, mybir.dt.from_np(a.dtype), kind="ExternalInput").ap()
            for n, a in arrays.items()]
    out = nc.dram_tensor("out_0", inputs["x"].shape, F32, kind="ExternalOutput").ap()
    hybrid_layer(nc, *args, out)
    result = run_bass_kernel_spmd(nc, [arrays], core_ids=[0])
    return result.results[0]["out_0"]
```

```python
import concourse.bass as bass
import numpy as np
from concourse import mybir

P = 128
F32 = mybir.dt.float32
F32R = mybir.dt.float32r
ALU = mybir.AluOpType
ACT = mybir.ActivationFunctionType
AX = mybir.AxisListType

SEQ, D_MODEL, D_FF, HEAD_DIM = 256, 2048, 8192, 128
TT = SEQ // P
HEADS = D_MODEL // HEAD_DIM
N_DIFF = HEADS // 2
HALF_DIM = HEAD_DIM // 2
KT = D_MODEL // P
KT_FF = D_FF // P
NC = 512
CHUNKS = D_MODEL // NC
CHUNKS_FF = D_FF // NC
KU = 2
SLOTS = 4
UPH = KT // KU
UPF = KT_FF // KU
U_OUT = UPH * HEADS
U_FF1 = U_OUT + UPH * CHUNKS
U_FF2 = U_FF1 + UPH * CHUNKS_FF
U_END = U_FF2 + UPF * CHUNKS
TPC = NC // P
WARM_UP = (6, 2, 2)
SPARE = 2
BY_TOK = SLOTS + SPARE

PIECES = [(tt, c) for tt in range(TT) for c in range(CHUNKS)]
LAST_PIECES = [(0, slice(0, 1024)), (0, slice(1024, 2048)), (1, slice(0, 512)),
               (1, slice(512, 1024)), (1, slice(1024, 1536)), (1, slice(1536, 1792)),
               (1, slice(1792, 2048))]

LAMBDA_INIT = 0.8 - 0.6
EPS = 1e-5
ALPHA = 2.0 ** 0.25
NEG = -1e30
ROPE_THETA = 10000.0
DILATION_CONFIGS = ((128, 1), (512, 4), (2048, 16))

KEYS = P + SEQ
T_ID = 0
T_ROPE_A = T_ID + P
T_ROPE_B = T_ROPE_A + 2 * TT * HALF_DIM
T_MASK_A = T_ROPE_B + 2 * TT * HEAD_DIM
T_MASK_B = T_MASK_A + KEYS
T_COLS = T_MASK_B + KEYS


def constant_table():
    table = np.zeros((P, T_COLS), np.float32)
    table[:, T_ID:T_ID + P] = np.eye(P, dtype=np.float32)
    for at, dim in ((T_ROPE_A, HALF_DIM), (T_ROPE_B, HEAD_DIM)):
        exponent = np.arange(0, dim, 2, dtype=np.float32) / np.float32(dim)
        inverse = np.float32(1.0) / np.power(np.float32(ROPE_THETA), exponent)
        angle = (np.arange(SEQ, dtype=np.float32)[:, None] * inverse[None, :]).astype(np.float32)
        cos, sin = np.cos(angle), np.sin(angle)
        whole = np.stack([np.concatenate([cos, cos], 1), np.concatenate([-sin, sin], 1)])
        whole = whole.reshape(2, TT, P, dim).transpose(2, 0, 1, 3)
        table[:, at:at + 2 * TT * dim] = whole.reshape(P, -1)
    t, u = np.arange(SEQ)[:, None], np.arange(SEQ)[None, :]
    causal = u <= t
    count = np.zeros((SEQ, SEQ))
    for window, dilation in DILATION_CONFIGS:
        count += causal & ((t - u) % dilation == 0) & (t - u <= window)
    for at, added in ((T_MASK_A, np.where(causal, 0.0, NEG)),
                      (T_MASK_B, np.where(count > 0, np.log(np.maximum(count, 1)), NEG))):
        table[:, at:at + P] = added[:P, :P]
        table[:, at + P:at + KEYS] = added[P:, :]
    return table


def keys_of(tt):
    return slice(0, P) if tt == 0 else slice(P, KEYS)


def hybrid_layer(nc, x, w_in, lq1, lk1, lq2, lk2, subln_g, w_out, ln1_g, ln1_b, w_ff1, w_ff2,
                 ln2_g, ln2_b, table, out):
    base = -(-nc.sbuf_base // 64) * 64
    KB = 1024

    def at(name, shape, dtype, offset):
        return nc.alloc_sbuf_tensor_at(name, shape, dtype, offset=base + offset)

    w_raw = at("w_raw", [P, SLOTS, KU * NC], F32, 0)
    w_hi = at("w_hi", [P, SLOTS, KU * NC], F32R, 16 * KB)
    w_lo = at("w_lo", [P, SLOTS, KU * NC], F32R, 32 * KB)
    relu = at("relu", [P, TT, NC], F32, 48 * KB)
    small = at("small", [P, 256], F32, 52 * KB)
    ident_t = at("ident_t", [P, P], F32, 53 * KB)
    X0 = 54 * KB
    x1T_hi = at("x1T_hi", [P, KT, SEQ], F32R, X0)
    x1T_lo = at("x1T_lo", [P, KT, SEQ], F32R, X0 + 16 * KB)
    late_hi = at("late_hi", [P, TPC, SEQ], F32R, X0)
    late_lo = at("late_lo", [P, TPC, SEQ], F32R, X0 + 4 * KB)
    y2 = at("y2", [P, TT, D_MODEL], F32, X0 + 8 * KB)
    H0 = X0 + 32 * KB
    EARLY = KT_FF - TPC
    hidT_hi = at("hidT_hi", [P, EARLY, SEQ], F32R, H0)
    hidT_lo = at("hidT_lo", [P, EARLY, SEQ], F32R, H0 + 60 * KB)
    zeros = at("zeros", [P, P], F32, H0)
    ln2_gb = at("ln2_gb", [P, 2, D_MODEL], F32, H0)
    mixT_hi = at("mixT_hi", [P, HEADS, SEQ], F32R, H0)
    mixT_lo = at("mixT_lo", [P, HEADS, SEQ], F32R, H0 + 16 * KB)
    xT_hi = at("xT_hi", [P, KT, SEQ], F32R, H0 + 32 * KB)
    xT_lo = at("xT_lo", [P, KT, SEQ], F32R, H0 + 48 * KB)
    ln1_gb = at("ln1_gb", [P, 2, D_MODEL], F32, H0 + 64 * KB)
    side_hi = at("side_hi", [P, SLOTS, KU * NC], F32R, H0 + 32 * KB)
    side_lo = at("side_lo", [P, SLOTS, KU * NC], F32R, H0 + 48 * KB)
    side_raw = at("side_raw", [P, SLOTS, KU * NC], F32, H0 + 80 * KB)
    A0 = H0 + 80 * KB
    tables = at("tables", [P, T_COLS - P], F32, A0)
    rope_cos = at("rope_cos", [P, TT, 2 * P], F32, A0 + 7 * KB)
    rope_sin = at("rope_sin", [P, TT, 2 * P], F32, A0 + 9 * KB)
    qk = at("qk", [P, TT, 2 * P], F32, A0 + 11 * KB)
    qkT = at("qkT", [P, 2, SEQ], F32, A0 + 13 * KB)
    v_sb = at("v_sb", [P, TT, P], F32, A0 + 15 * KB)
    scores = at("scores", [P, 2, KEYS], F32, A0 + 16 * KB)
    probs = at("probs", [P, 2, KEYS], F32, A0 + 19 * KB)
    y1 = at("y1", [P, TT, D_MODEL], F32, A0 + 24 * KB)
    final_probs = at("final_probs", [P, KEYS], F32, 48 * KB)
    probsT = at("probsT", [P, KEYS], F32, 48 * KB + 1536)
    o_sb = at("o_sb", [P, TT, P], F32, 48 * KB + 3072)
    squares = at("squares", [P, TT, P], F32, A0 + 22 * KB)

    def part(first, n):
        return small[:, first:first + n]

    neg_max, row_sum, inv_sum = part(0, 4), part(4, 4), part(8, 4)
    diff_scale, sum_sq, o_scale = part(12, 2), part(14, 2), part(16, 2)
    mean_sq, root = part(18, 2), part(20, 2)
    minus_half, subln = part(22, 2), part(24, 1)
    subln_scaled, neg_lam, lam_sum, lam_exp = part(25, 1), part(26, 1), part(28, 2), part(30, 2)
    mean_var, inv_std, var_eps = part(32, 4), part(36, 2), part(38, 2)
    eps_sum = part(42, 2)
    stats = part(48, TT * CHUNKS * 6)
    lam_in = at("lam_in", [P, 4, HALF_DIM], F32, A0 + 23 * KB)
    lam_prod = at("lam_prod", [P, 2, HALF_DIM], F32, H0 + 64 * KB)

    spare_out_hi = at("spare_out_hi", [P, SPARE, KU * NC], F32R, X0 + 8 * KB)
    spare_ff2_hi = at("spare_ff2_hi", [P, SPARE, KU * NC], F32R, H0 + 16 * KB)
    spare_lo = at("spare_lo", [P, SPARE, KU * NC], F32R, X0 + 24 * KB)

    spill = nc.dram_tensor("ln1_spill", [P, TT, D_MODEL], F32).ap()

    def bank(name, first, count):
        return nc.alloc_psum_tensor(name, [P, count, NC], F32)

    proj_ps = [bank("proj_even", 0, TT), bank("proj_odd", 2, TT)]
    acc_ps = proj_ps[0]
    scores_ps = bank("scores_ps", 4, 2)
    turn_ps = bank("turn_ps", 6, 1)
    out_ps = bank("out_ps", 7, 1)
    piece_ps = [scores_ps[:, 0, :], scores_ps[:, 1, :], turn_ps[:, 0, :], out_ps[:, 0, :]]

    sems = {}

    def sem(name):
        sems[name] = nc.alloc_semaphore(name)
        return sems[name]

    w_loaded = [sem(f"w_loaded{s}") for s in range(SLOTS)]
    side_loaded = [sem(f"side_loaded{s}") for s in range(SLOTS)]
    side_rounded, side_split = sem("side_rounded"), sem("side_split")
    w_rounded, w_split, w_used = sem("w_rounded"), sem("w_split"), sem("w_used")
    ident_loaded, tables_loaded = sem("ident_loaded"), sem("tables_loaded")
    x_loaded = [sem(f"x_loaded{k}") for k in range(UPH)]
    lam_loaded, gb1_loaded, gb2_loaded = sem("lam_loaded"), sem("gb1_loaded"), sem("gb2_loaded")
    lam_mult, lam_summed, lam_exped, lam_ready = (
        sem("lam_mult"), sem("lam_summed"), sem("lam_exped"), sem("lam_ready"))
    powers_ready, zeroed = sem("powers_ready"), sem("zeroed")
    turned, turn_rounded, turn_split = sem("turned"), sem("turn_rounded"), sem("turn_split")
    proj_done, v_copied = sem("proj_done"), sem("v_copied")
    rope_terms, roped = sem("rope_terms"), sem("roped")
    qk_turned, qkT_copied = sem("qk_turned"), sem("qkT_copied")
    scores_done, masked, max_found = sem("scores_done"), sem("masked"), sem("max_found")
    exp_done, sum_inverted = sem("exp_done"), sem("sum_inverted")
    diff_scaled, combined = sem("diff_scaled"), sem("combined")
    probs_turned, probsT_copied = sem("probs_turned"), sem("probsT_copied")
    pv_done, squared = sem("pv_done"), sem("squared")
    mean_ready, root_ready, scale_ready = sem("mean_ready"), sem("root_ready"), sem("scale_ready")
    o_ready, o_turned = sem("o_ready"), sem("o_turned")
    mix_rounded, mix_split = sem("mix_rounded"), sem("mix_split")
    out_done, y1_summed, y1_stats = sem("out_done"), sem("y1_summed"), sem("y1_stats")
    moments, var_ready, std_ready = sem("moments"), sem("var_ready"), sem("std_ready")
    centred, x1_ready, spilled = sem("centred"), sem("x1_ready"), sem("spilled")
    ff1_done, relu_done, hid_squared = sem("ff1_done"), sem("relu_done"), sem("hid_squared")
    hid_turned, hid_rounded, hid_split = sem("hid_turned"), sem("hid_rounded"), sem("hid_split")
    x1_back = sem("x1_back")
    ff2_done, y2_summed, y2_stats = sem("ff2_done"), sem("y2_summed"), sem("y2_stats")
    y2_ready, stored = sem("y2_ready"), sem("stored")

    x_d = x.rearrange("b (t p) d -> p (b t) d", p=P)
    out_d = out.rearrange("b (t p) d -> p (b t) d", p=P)
    w_in_d = w_in.rearrange("l (u k p) (g s h d) -> p (l u) k g s h d", k=KU, p=P, g=2, s=3,
                            d=HEAD_DIM)

    def by_unit(w):
        return w.rearrange("l (u k p) (c n) -> p (l u) k c n", k=KU, p=P, n=NC)

    w_out_d, w_ff1_d, w_ff2_d = by_unit(w_out), by_unit(w_ff1), by_unit(w_ff2)

    def one(i):
        return bass.ds(i, 1)

    HC = 3 * HEAD_DIM

    def load_head_unit(sp, kind, h, head, k, first_lap=False):
        slot = k % SLOTS
        if not first_lap:
            sp.wait_ge(w_split, UPH * h + k - (SLOTS - 1))
        dst = w_raw[:, slot, 0:KU * HC].rearrange("p (k s d) -> p k s d", k=KU, s=3)
        for kk in range(KU):
            src = w_in_d[:, k, kk, kind, :, one(head), :].rearrange("p s h d -> p s (h d)")
            sp.dma_start(dst[:, kk], src).then_inc(w_loaded[slot], 16)

    def load_chunk_unit(sp, w, u, row, chunk, slot, back=SLOTS):
        sp.wait_ge(w_split, u - (back - 1))
        dst = w_raw[:, slot, :].rearrange("p (k n) -> p k n", k=KU)
        src = w[:, row, :, chunk, :] if isinstance(chunk, int) else (
            w[:, row, :, one(chunk), :].rearrange("p k c n -> p k (c n)"))
        sp.dma_start(dst, src).then_inc(w_loaded[slot], 16)

    def sync_program(sp):
        for k in range(UPH):
            cols = slice(k * KU * P, (k + 1) * KU * P)
            sp.dma_start(y1[:, :, cols], x_d[:, :, cols]).then_inc(x_loaded[k], 16)
            load_head_unit(sp, 0, 0, 0, k, first_lap=k < SLOTS)
        for kind in range(2):
            first = 1 if kind == 0 else 0
            with sp.Fori(first, N_DIFF) as j:
                for k in range(UPH):
                    load_head_unit(sp, kind, j + N_DIFF * kind, j, k)
        with sp.Fori(0, CHUNKS - 1) as n:
            for k in range(UPH):
                load_chunk_unit(sp, w_out_d, UPH * n + (U_OUT + k), k, n, k % SLOTS)
        sp.wait_ge(w_used, U_OUT + UPH)
        for k in range(SLOTS):
            sp.dma_start(side_raw[:, k, :].rearrange("p (k n) -> p k n", k=KU),
                         w_ff1_d[:, k, :, 0, :]).then_inc(side_loaded[k], 16)
        for k in range(UPH):
            load_chunk_unit(sp, w_out_d, U_OUT + UPH * (CHUNKS - 1) + k, k, CHUNKS - 1, k % SLOTS)
        for k in range(SLOTS, UPH):
            load_chunk_unit(sp, w_ff1_d, U_FF1 + k, k, 0, k % SLOTS, back=2 * SLOTS)
        with sp.Fori(1, CHUNKS_FF) as n:
            for k in range(UPH):
                load_chunk_unit(sp, w_ff1_d, UPH * n + (U_FF1 + k), k, n, k % SLOTS)
        with sp.Fori(0, CHUNKS - 1) as n:
            with sp.Fori(0, UPF // SLOTS) as lap:
                for k in range(SLOTS):
                    load_ff2_unit(sp, UPF * n + SLOTS * lap + (U_FF2 + k), SLOTS * lap + k, n, k)
        for k in range(UPF):
            load_ff2_unit(sp, U_FF2 + UPF * (CHUNKS - 1) + k, k, CHUNKS - 1, k % SLOTS)
            if k == UPF * 3 // 4:
                sp.wait_ge(w_used, U_FF2 + UPF * (CHUNKS - 1) + UPF // 2)
                for n, v in enumerate((ln2_g, ln2_b)):
                    sp.dma_start(ln2_gb[:, n, :], v.partition_broadcast(P).rearrange(
                        "p l d -> p (l d)")).then_inc(gb2_loaded, 16)
        for i, (tt, cols) in enumerate(LAST_PIECES):
            sp.wait_ge(y2_ready, i + 1)
            sp.dma_start(out_d[:, tt, cols], y2[:, tt, cols]).then_inc(stored, 16)
        sp.wait_ge(stored, 16 * len(LAST_PIECES))

    def load_ff2_unit(sp, u, row, chunk, slot):
        sp.wait_ge(w_split, u - (SLOTS - 1))
        dst = w_raw[:, slot, :].rearrange("p (k n) -> p k n", k=KU)
        if isinstance(row, int):
            src = w_ff2_d[:, row, :, chunk, :]
        else:
            src = w_ff2_d[:, one(row), :, one(chunk), :].rearrange("p u k c n -> p (u k) (c n)")
        sp.dma_start(dst, src).then_inc(w_loaded[slot], 16)

    def tensor_program(pe):
        def warm_up(count):
            for _ in range(count):
                pe.matmul(proj_ps[1][:, 0, 0:P], zeros[:, :], zeros[:, :], start=True, stop=True)

        def transpose_x(i):
            pe.wait_ge(x_loaded[i], 16)
            if i >= 4:
                pe.wait_ge(turn_split, i - 3)
            for t in range(KU):
                for tt in range(TT):
                    k = i * KU + t
                    ins = pe.transpose(piece_ps[i % 4][:, t * SEQ + tt * P:t * SEQ + (tt + 1) * P],
                                       y1[:, tt, k * P:(k + 1) * P], ident_t[:, :])
            ins.then_inc(turned, 1)

        def transpose_piece(i):
            tt, c = PIECES[i]
            pe.wait_ge(x1_ready, i + 1)
            if i >= 4:
                pe.wait_ge(turn_split, UPH + i - 3)
            for t in range(TPC):
                k = c * TPC + t
                ins = pe.transpose(piece_ps[i % 4][:, t * P:(t + 1) * P],
                                   y1[:, tt, k * P:(k + 1) * P], ident_t[:, :])
            ins.then_inc(turned, 1)

        def half_products(k, home, left_hi, left_lo, acc, cols, kts, tt):
            right_hi, right_lo, slot = home
            toks = slice(tt * P, (tt + 1) * P)
            for kk in range(KU):
                t = KU * k + kk
                hi, lo = left_hi(t), left_lo(t)
                w = slice(kk * cols, (kk + 1) * cols)
                pe.matmul(acc[:, tt, 0:cols], hi[:, toks], right_hi[:, slot, w],
                          start=(t == 0), stop=False)
                pe.matmul(acc[:, tt, 0:cols], hi[:, toks], right_lo[:, slot, w],
                          start=False, stop=False)
                ins = pe.matmul(acc[:, tt, 0:cols], lo[:, toks], right_hi[:, slot, w],
                                start=False, stop=(t == kts - 1))
            return ins

        def products(u, k, left_hi, left_lo, acc, cols, kts, free=None, tok_done=None, tts=(0, 1),
                     between=None, home=None):
            if home is not None and home[0] is side_hi:
                pe.wait_ge(side_split, k + 1)
            else:
                pe.wait_ge(w_split, u + 1)
            for tt in tts:
                if free is not None and k == 0:
                    free(tt)
                ins = half_products(k, home or (w_hi, w_lo, k % SLOTS), left_hi, left_lo, acc, cols,
                                    kts, tt)
                if tt == TT - 1:
                    ins.then_inc(w_used, 1)
                elif tok_done is not None and KU * (k + 1) == kts:
                    ins.then_inc(tok_done, 1)
                if tt == 0 and between is not None:
                    between()

        def tok_by_tok(unit, first, count, inside=None):
            for tt in range(TT):
                for k in range(first, first + count):
                    unit(k, tts=(tt,))
                    if inside and (tt, k) in inside:
                        inside[tt, k]()

        def turn_qk(h):
            pe.wait_ge(roped, h + 1)
            for s in range(2):
                for tt in range(TT):
                    ins = pe.transpose(turn_ps[:, 0, s * SEQ + tt * P:s * SEQ + (tt + 1) * P],
                                       qk[:, tt, s * P:(s + 1) * P], ident_t[:, :])
            ins.then_inc(qk_turned, 1)

        def score(h, maps):
            pe.wait_ge(qkT_copied, h + 1)
            width = P // maps
            for m in range(maps):
                rows = slice(m * width, (m + 1) * width)
                for tt in range(TT):
                    ins = pe.matmul(scores_ps[:, m, keys_of(tt)], qkT[rows, 0, tt * P:(tt + 1) * P],
                                    qkT[rows, 1, 0:(tt + 1) * P], start=True, stop=True)
            ins.then_inc(scores_done, 1)

        def turn_probs(h):
            pe.wait_ge(combined, h + 1)
            if not (isinstance(h, int) and h == 0):
                pe.wait_ge(mix_split, h)
            for b in range(3):
                ins = pe.transpose(out_ps[:, 0, b * P:(b + 1) * P], final_probs[:, b * P:(b + 1) * P],
                                   ident_t[:, :])
            ins.then_inc(probs_turned, 1)

        def weigh_values(h, maps):
            pe.wait_ge(probsT_copied, h + 1)
            for tt, key_tile, block in ((0, 0, 0), (1, 0, 1), (1, 1, 2)):
                first = (0 if maps == 2 else SEQ) + tt * P
                weights, values = probsT[:, block * P:(block + 1) * P], v_sb[:, key_tile, :]
                left, right = (weights, values) if maps == 2 else (values, weights)
                ins = pe.matmul(out_ps[:, 0, first:first + P], left, right,
                                start=(key_tile == 0), stop=(key_tile == tt))
            ins.then_inc(pv_done, 1)

        def turn_output(h):
            pe.wait_ge(o_ready, h + 1)
            for tt in range(TT):
                ins = pe.transpose(out_ps[:, 0, SEQ + tt * P:SEQ + (tt + 1) * P], o_sb[:, tt, :],
                                   ident_t[:, :])
            ins.then_inc(o_turned, 1)

        def slot(h, att_maps, turns_out, unit):
            for k in range(UPH):
                unit(k)
                if k == 0 and turns_out:
                    turn_output(h - 2)
                if k == 1 and att_maps:
                    turn_qk(h - 1)
                if k == 2 and att_maps:
                    score(h - 1, att_maps)
                if k == 5 and att_maps:
                    turn_probs(h - 1)
                if k == 6 and att_maps:
                    weigh_values(h - 1, att_maps)

        def head_slot(h, parity, att_maps, turns_out):
            acc = proj_ps[parity]

            def unit(k):
                if k == 0 and not (isinstance(h, int) and h < 2):
                    pe.wait_ge(roped, h - 1)
                if isinstance(h, int) and h == 0:
                    for i in {0: (0, 1), 1: (2, 3)}.get(k, (k + 2,)):
                        if i < UPH:
                            transpose_x(i)
                        if i < 2:
                            warm_up(WARM_UP[i + 1])
                    pe.wait_ge(turn_split, k + 1)
                products(UPH * h + k, k, lambda i: xT_hi[:, i, :], lambda i: xT_lo[:, i, :], acc, HC,
                         KT)

            slot(h, att_maps, turns_out, unit)

        pe.wait_ge(zeroed, 1)
        warm_up(WARM_UP[0])
        pe.wait_ge(ident_loaded, 16)
        head_slot(0, 0, 0, False)
        head_slot(1, 1, 2, False)
        with pe.Fori(1, N_DIFF // 2) as j:
            head_slot(2 * j, 0, 2, True)
            head_slot(2 * j + 1, 1, 2, True)
        head_slot(N_DIFF, 0, 2, True)
        head_slot(N_DIFF + 1, 1, 1, True)
        with pe.Fori(N_DIFF // 2 + 1, HEADS // 2) as j:
            head_slot(2 * j, 0, 1, False)
            head_slot(2 * j + 1, 1, 1, False)

        def out_unit(n, k, tts=(0, 1), between=None):
            def free(tt):
                if isinstance(n, int) and n == 0:
                    pe.wait_ge(roped, HEADS - 1)
                else:
                    pe.wait_ge(y1_summed, TT * n - TT + tt + 1)
            spare = isinstance(n, int) and n == CHUNKS - 1 and k >= UPH - SPARE
            products(UPH * n + (U_OUT + k), k, lambda i: mixT_hi[:, i, :],
                     lambda i: mixT_lo[:, i, :], acc_ps, NC, KT, free, out_done, tts, between,
                     (spare_out_hi, spare_lo, k - (UPH - SPARE)) if spare else None)

        for k in range(UPH):
            if k == UPH - 1:
                pe.wait_ge(mix_split, HEADS)
            out_unit(0, k, between={2: lambda: score(HEADS - 1, 1),
                                    5: lambda: weigh_values(HEADS - 1, 1)}.get(k))
            if k == 1:
                turn_qk(HEADS - 1)
            if k == 4:
                turn_probs(HEADS - 1)
        with pe.Fori(1, CHUNKS - 1) as n:
            for k in range(UPH):
                out_unit(n, k)
        for k in range(UPH - BY_TOK):
            out_unit(CHUNKS - 1, k)
        after = {(1, UPH - 4): 0, (1, UPH - 2): 1}
        tok_by_tok(lambda k, tts: out_unit(CHUNKS - 1, k, tts), UPH - BY_TOK, BY_TOK,
                   {when: lambda i=i: transpose_piece(i) for when, i in after.items()})

        def ff1_unit(i, k, tts=(0, 1), home=None):
            def free(tt):
                if isinstance(i, int) and i == 0:
                    pe.wait_ge(y1_summed, TT * CHUNKS - TT + tt + 1)
                else:
                    pe.wait_ge(relu_done, TT * i - TT + tt + 1)
            products(UPH * i + (U_FF1 + k), k, lambda t: x1T_hi[:, t, :],
                     lambda t: x1T_lo[:, t, :], acc_ps, NC, KT, free, ff1_done, tts,
                     home=home)

        def first_ff1_unit(k, tts=(0, 1)):
            for tt in tts:
                pe.wait_ge(turn_split, UPH + PIECES.index((tt, KU * k // TPC)) + 1)
            ff1_unit(0, k, tts, (side_hi, side_lo, k) if k < SLOTS else None)

        def turn_hidden(i):
            pe.wait_ge(hid_squared, i + 1)
            dst = scores_ps.rearrange("p b n -> p (b n)")
            for t in range(TPC):
                for tt in range(TT):
                    ins = pe.transpose(dst[:, t * SEQ + tt * P:t * SEQ + (tt + 1) * P],
                                       relu[:, tt, t * P:(t + 1) * P], ident_t[:, :])
            ins.then_inc(hid_turned, 1)

        after = {(0, 0): 2, (0, 2): 3, (0, 5): 4, (1, 0): 5, (1, 1): 6, (1, 3): 7}
        tok_by_tok(first_ff1_unit, 0, UPH,
                   {when: lambda i=i: transpose_piece(i) for when, i in after.items()})
        with pe.Fori(1, CHUNKS_FF) as i:
            for k in range(UPH):
                ff1_unit(i, k)
                if k == 1:
                    turn_hidden(i - 1)

        def hid(early, late):
            return lambda t: early[:, t, :] if t < EARLY else late[:, t - EARLY, :]

        def ff2_unit(n, k, tts=(0, 1)):
            def free(tt):
                if isinstance(n, int) and n == 0:
                    pe.wait_ge(relu_done, TT * CHUNKS_FF - TT + tt + 1)
                else:
                    pe.wait_ge(y2_summed, TT * n - TT + tt + 1)
            spare = isinstance(n, int) and n == CHUNKS - 1 and k >= UPF - SPARE
            products(UPF * n + (U_FF2 + k), k, hid(hidT_hi, late_hi), hid(hidT_lo, late_lo), acc_ps,
                     NC, KT_FF, free, ff2_done, tts,
                     home=(spare_ff2_hi, spare_lo, k - (UPF - SPARE)) if spare else None)

        for k in range(UPF):
            if KU * k == EARLY:
                pe.wait_ge(hid_split, CHUNKS_FF)
            ff2_unit(0, k)
            if k == 1:
                turn_hidden(CHUNKS_FF - 1)
        with pe.Fori(1, CHUNKS - 1) as n:
            for k in range(UPF):
                ff2_unit(n, k)
        for k in range(UPF - BY_TOK):
            ff2_unit(CHUNKS - 1, k)
        tok_by_tok(lambda k, tts: ff2_unit(CHUNKS - 1, k, tts), UPF - BY_TOK, BY_TOK)

    def scalar_program(act):
        def round_unit(u, slot, lap, cols, fresh=False, back=SLOTS, units=1):
            if cols == KU * HC:
                loads = KU * lap
            else:
                loads = lap + (KU - 1) * (U_OUT // SLOTS)
            act.wait_ge(w_loaded[slot], 16 * loads)
            if not fresh:
                act.wait_ge(w_used, u - (back - 1))
            act.activation(w_hi[:, slot, 0:cols], w_raw[:, slot, 0:cols], ACT.Copy).then_inc(
                w_rounded, units)

        def round_spare(n, slot, lap, hi):
            act.wait_ge(w_loaded[slot], 16 * (lap + (KU - 1) * (U_OUT // SLOTS)))
            act.activation(hi[:, n, :], w_raw[:, slot, :], ACT.Copy).then_inc(w_rounded, 1)

        def ahead(first, k, cols=KU * NC):
            round_unit(first + (k + SLOTS), k % SLOTS, first // SLOTS + (k // SLOTS + 2), cols)

        def ahead_mlp(first, k, back=SLOTS, units=1):
            round_unit(first + (k + SLOTS), k % SLOTS, first // SLOTS + (k // SLOTS + 1), KU * NC,
                       back=back, units=units)

        def round_x(i):
            act.wait_ge(turned, i + 1)
            act.activation(xT_hi[:, i * KU:(i + 1) * KU, :].rearrange("p k t -> p (k t)"),
                           piece_ps[i % 4], ACT.Copy).then_inc(turn_rounded, 1)

        def copy_v(h, parity):
            act.wait_ge(w_used, UPH * h + UPH)
            act.activation(v_sb[:, :, :], proj_ps[parity][:, :, 2 * P:3 * P], ACT.Copy).then_inc(
                v_copied, 1)

        def copy_qkT(h):
            act.wait_ge(qk_turned, h + 1)
            act.activation(qkT[:, :, :].rearrange("p s t -> p (s t)"), turn_ps[:, 0, :],
                           ACT.Copy).then_inc(qkT_copied, 1)

        def exponentials(h, maps):
            act.wait_ge(max_found, 2 * h + 2)
            for tt in range(TT):
                for m in range(maps):
                    i = 2 * tt + m
                    ins = act.activation(probs[:, m, keys_of(tt)], scores[:, m, keys_of(tt)], ACT.Exp,
                                         bias=neg_max[:, i:i + 1], accum_out=row_sum[:, i:i + 1])
            ins.then_inc(exp_done, 1)

        def copy_probsT(h):
            act.wait_ge(probs_turned, h + 1)
            act.activation(probsT[:, :], out_ps[:, 0, 0:KEYS], ACT.Copy).then_inc(probsT_copied, 1)

        def square_sums(h):
            act.wait_ge(pv_done, h + 1)
            act.wait_ge(sum_inverted, h + 1)
            for tt in range(TT):
                ins = act.activation(squares[:, tt, :], out_ps[:, 0, tt * P:(tt + 1) * P], ACT.Square,
                                     scale=inv_sum[:, 2 * tt:2 * tt + 1],
                                     accum_out=sum_sq[:, tt:tt + 1])
            ins.then_inc(squared, 1)

        def scale_output(h):
            act.wait_ge(scale_ready, h + 1)
            for tt in range(TT):
                ins = act.activation(o_sb[:, tt, :], out_ps[:, 0, tt * P:(tt + 1) * P], ACT.Copy,
                                     scale=o_scale[:, tt:tt + 1])
            ins.then_inc(o_ready, 1)

        def round_mix(h, maps):
            if maps == 2:
                act.wait_ge(o_turned, h + 1)
            else:
                act.wait_ge(pv_done, h + 1)
            dst = mixT_hi[:, h, :] if isinstance(h, int) else (
                mixT_hi[:, one(h), :].rearrange("p h t -> p (h t)"))
            act.activation(dst, out_ps[:, 0, SEQ:2 * SEQ], ACT.Copy,
                           scale=subln_scaled if maps == 2 else 1.0).then_inc(mix_rounded, 1)

        def slot(h, parity, att_maps, out_maps):
            cols = KU * HC
            first = UPH * h
            ahead(first, 0, cols)
            if out_maps:
                round_mix(h - 2, out_maps)
            ahead(first, 1, cols)
            if att_maps:
                copy_qkT(h - 1)
            ahead(first, 2, cols)
            if att_maps:
                exponentials(h - 1, att_maps)
            ahead(first, 3, cols)
            cols = KU * NC if isinstance(h, int) and h == HEADS - 1 else cols
            ahead(first, 4, cols)
            ahead(first, 5, cols)
            if att_maps:
                copy_probsT(h - 1)
            ahead(first, 6, cols)
            if att_maps == 2:
                square_sums(h - 1)
            copy_v(h, parity)
            ahead(first, 7, cols)
            if att_maps == 2:
                scale_output(h - 1)

        for k in range(SLOTS):
            round_x(k)
            round_unit(k, k, 1, KU * HC, fresh=True)
        for k in range(SLOTS):
            round_x(SLOTS + k)
            ahead(0, k, KU * HC)
        for k in range(SLOTS, UPH):
            if k == UPH - 2:
                act.wait_ge(lam_loaded, 16 * 5)
                act.activation(subln_scaled, subln, ACT.Copy,
                               scale=(1.0 - LAMBDA_INIT) * HEAD_DIM ** 0.5)
                act.wait_ge(lam_summed, 2)
                act.activation(lam_exp, lam_sum, ACT.Exp).then_inc(lam_exped, 1)
            if k == UPH - 1:
                copy_v(0, 0)
            ahead(0, k, KU * HC)
        slot(1, 1, 2, 0)
        with act.Fori(1, N_DIFF // 2) as j:
            slot(2 * j, 0, 2, 2)
            slot(2 * j + 1, 1, 2, 2)
        slot(N_DIFF, 0, 2, 2)
        slot(N_DIFF + 1, 1, 1, 2)
        with act.Fori(N_DIFF // 2 + 1, HEADS // 2 - 1) as j:
            slot(2 * j, 0, 1, 1)
            slot(2 * j + 1, 1, 1, 1)
        slot(HEADS - 2, 0, 1, 1)
        slot(HEADS - 1, 1, 1, 1)

        round_mix(HEADS - 2, 1)
        ahead(U_OUT, 0)
        copy_qkT(HEADS - 1)
        ahead(U_OUT, 1)
        exponentials(HEADS - 1, 1)
        ahead(U_OUT, 2)
        ahead(U_OUT, 3)
        ahead(U_OUT, 4)
        copy_probsT(HEADS - 1)
        round_mix(HEADS - 1, 1)
        ahead(U_OUT, 5)
        ahead(U_OUT, 6)
        ahead(U_OUT, 7)
        with act.Fori(1, CHUNKS - 1) as n:
            for k in range(UPH):
                ahead(UPH * n + U_OUT, k)

        def round_piece(i):
            tt, c = PIECES[i]
            act.wait_ge(turned, UPH + i + 1)
            act.activation(x1T_hi[:, c * TPC:(c + 1) * TPC, tt * P:(tt + 1) * P],
                           piece_ps[i % 4].rearrange("p (k t) -> p k t", k=TPC),
                           ACT.Copy).then_inc(turn_rounded, 1)

        last_out = U_OUT + UPH * (CHUNKS - 1)

        def round_side(k):
            act.wait_ge(side_loaded[k], 16)
            act.activation(side_hi[:, k, :], side_raw[:, k, :], ACT.Copy).then_inc(side_rounded, 1)

        ahead(last_out, 0)
        round_side(0)
        ahead(last_out, 1)
        for n in range(SPARE):
            round_spare(n, n + SLOTS - SPARE, U_FF1 // SLOTS, spare_out_hi)
        for k in range(1, SLOTS):
            round_side(k)
        for k in range(SLOTS):
            round_piece(k)
            ahead_mlp(U_FF1, k, back=2 * SLOTS, units=SLOTS + 1 if k == 0 else 1)
        for i in range(SLOTS, len(PIECES)):
            round_piece(i)

        def relu_chunk(i, tts=(0, 1)):
            for tt in tts:
                if tt == 0:
                    act.wait_ge(ff1_done, i + 1)
                else:
                    act.wait_ge(w_used, UPH * i + (U_FF1 + UPH))
                if not (isinstance(i, int) and i == 0):
                    act.wait_ge(hid_turned, i)
                act.activation(relu[:, tt, :], acc_ps[:, tt, :], ACT.Relu).then_inc(relu_done, 1)

        def round_hidden(i, last=False):
            act.wait_ge(hid_turned, i + 1)
            dst = late_hi if last else hidT_hi[:, bass.ds(i * TPC, TPC), :]
            act.activation(dst.rearrange("p k t -> p (k t)"),
                           scores_ps.rearrange("p b n -> p (b n)"), ACT.Copy).then_inc(hid_rounded, 1)

        relu_chunk(0, (0,))
        for k in range(SLOTS, UPH - 1):
            ahead_mlp(U_FF1, k)
        relu_chunk(0, (1,))
        ahead_mlp(U_FF1, UPH - 1)
        with act.Fori(1, CHUNKS_FF) as i:
            for k in range(UPH):
                if k == 2:
                    round_hidden(i - 1)
                if k == UPH - 1:
                    relu_chunk(i)
                ahead_mlp(UPH * i + U_FF1, k)

        for k in range(SLOTS):
            if k == 2:
                round_hidden(CHUNKS_FF - 1, last=True)
            ahead_mlp(U_FF2, k)
        last_lap = (U_END - U_FF2) // SLOTS - 2
        with act.Fori(1, last_lap) as lap:
            for k in range(SLOTS):
                ahead_mlp(SLOTS * lap + U_FF2, k)
        for k in range(SLOTS - SPARE):
            ahead_mlp(SLOTS * last_lap + U_FF2, k)
        for n in range(SPARE):
            round_spare(n, n + SLOTS - SPARE, U_END // SLOTS - 1, spare_ff2_hi)

    def vector_program(dve):
        def split_unit(u, slot, cols, units=1):
            dve.wait_ge(w_rounded, u + 1)
            dve.tensor_tensor(w_lo[:, slot, 0:cols], w_raw[:, slot, 0:cols],
                              w_hi[:, slot, 0:cols].bitcast(F32),
                              ALU.subtract).then_inc(w_split, units)

        def split_spare(n, u, slot, hi):
            dve.wait_ge(w_rounded, u + 1)
            dve.tensor_tensor(spare_lo[:, n, :], w_raw[:, slot, :], hi[:, n, :].bitcast(F32),
                              ALU.subtract).then_inc(w_split, 1)

        def ahead(first, k, cols=KU * NC, units=1):
            split_unit(first + (k + SLOTS), k % SLOTS, cols, units)

        def split_x(i):
            dve.wait_ge(turn_rounded, i + 1)
            hi, lo = (t[:, i * KU:(i + 1) * KU, :].rearrange("p k t -> p (k t)")
                      for t in (xT_hi, xT_lo))
            dve.tensor_tensor(lo, piece_ps[i % 4], hi.bitcast(F32), ALU.subtract).then_inc(
                turn_split, 1)

        def rope(h, parity, maps):
            width = P // maps
            half = width // 2
            groups = 2 * maps
            t0 = (T_ROPE_A if maps == 2 else T_ROPE_B) - P
            tabs = tables[:, t0:t0 + 2 * TT * width].rearrange("p (c t d) -> p c t d", c=2, t=TT)

            def grouped(ap):
                return ap.rearrange("p t (g d) -> p t g d", g=groups)

            def spread(ap):
                return ap.unsqueeze(2).to_broadcast([P, TT, groups, ap.shape[-1]])

            src = grouped(proj_ps[parity][:, :, 0:2 * P])
            sin = tabs[:, 1]
            dve.wait_ge(v_copied, h + 1)
            dve.tensor_tensor(grouped(rope_cos[:, :, :]), src, spread(tabs[:, 0]),
                              ALU.mult).then_inc(rope_terms, 1)
            dve.tensor_tensor(grouped(rope_sin[:, :, :])[:, :, :, 0:half], src[:, :, :, half:width],
                              spread(sin[:, :, 0:half]), ALU.mult).then_inc(rope_terms, 1)
            dve.tensor_tensor(grouped(rope_sin[:, :, :])[:, :, :, half:width], src[:, :, :, 0:half],
                              spread(sin[:, :, half:width]), ALU.mult).then_inc(rope_terms, 1)
            dve.wait_ge(rope_terms, 3 * h + 3)
            dve.tensor_tensor(qk[:, :, :], rope_cos[:, :, :], rope_sin[:, :, :],
                              ALU.add).then_inc(roped, 1)

        def mask_and_max(h, maps):
            t0 = (T_MASK_A if maps == 2 else T_MASK_B) - P
            mask = tables[:, t0:t0 + KEYS].unsqueeze(1).to_broadcast([P, maps, KEYS])
            scale = float((P // maps) ** -0.5)
            dve.wait_ge(scores_done, h + 1)
            dve.scalar_tensor_tensor(out=scores[:, 0:maps, :], in0=scores_ps[:, 0:maps, 0:KEYS],
                                     scalar=scale, in1=mask, op0=ALU.mult,
                                     op1=ALU.add).then_inc(masked, 1)
            dve.wait_ge(masked, h + 1)
            for tt in range(TT):
                dve.tensor_reduce(neg_max[:, 2 * tt:2 * tt + maps], scores[:, 0:maps, keys_of(tt)],
                                  AX.X, ALU.max, negate=True).then_inc(max_found, 1)

        def invert_sums(h, maps):
            dve.wait_ge(exp_done, h + 1)
            if maps == 2:
                dve.reciprocal(inv_sum[:, :], row_sum[:, :]).then_inc(sum_inverted, 1)
            else:
                dve.reciprocal(inv_sum[:, 0:4:2], row_sum[:, 0:4:2]).then_inc(sum_inverted, 1)

        def combine(h, maps):
            dve.wait_ge(sum_inverted, h + 1)
            if maps == 1:
                for tt in range(TT):
                    ins = dve.tensor_scalar(final_probs[:, keys_of(tt)], probs[:, 0, keys_of(tt)],
                                            inv_sum[:, 2 * tt:2 * tt + 1], None, ALU.mult)
                ins.then_inc(combined, 1)
                return
            dve.scalar_tensor_tensor(out=diff_scale, in0=row_sum[:, 0:4:2], scalar=neg_lam,
                                     in1=inv_sum[:, 1:4:2], op0=ALU.mult,
                                     op1=ALU.mult).then_inc(diff_scaled, 1)
            dve.wait_ge(diff_scaled, h + 1)
            for tt in range(TT):
                ins = dve.scalar_tensor_tensor(
                    out=final_probs[:, keys_of(tt)], in0=probs[:, 1, keys_of(tt)],
                    scalar=diff_scale[:, tt:tt + 1], in1=probs[:, 0, keys_of(tt)],
                    op0=ALU.mult, op1=ALU.add)
            ins.then_inc(combined, 1)

        def split_mix(h, maps):
            dve.wait_ge(mix_rounded, h + 1)

            def row(t):
                return t[:, h, :] if isinstance(h, int) else (
                    t[:, one(h), :].rearrange("p h t -> p (h t)"))
            src, hi, lo = out_ps[:, 0, SEQ:2 * SEQ], row(mixT_hi).bitcast(F32), row(mixT_lo)
            if maps == 2:
                dve.scalar_tensor_tensor(out=lo, in0=src, scalar=subln_scaled, in1=hi, op0=ALU.mult,
                                         op1=ALU.subtract).then_inc(mix_split, 1)
            else:
                dve.tensor_tensor(lo, src, hi, ALU.subtract).then_inc(mix_split, 1)

        def slot(h, parity, maps, att_maps, out_maps):
            cols = KU * HC
            first = UPH * h
            ahead(first, 0, cols)
            if out_maps:
                split_mix(h - 2, out_maps)
            ahead(first, 1, cols)
            if att_maps:
                mask_and_max(h - 1, att_maps)
            ahead(first, 2, cols)
            if att_maps:
                invert_sums(h - 1, att_maps)
                combine(h - 1, att_maps)
            ahead(first, 3, cols)
            cols = KU * NC if isinstance(h, int) and h == HEADS - 1 else cols
            ahead(first, 4, cols)
            ahead(first, 5, cols)
            ahead(first, 6, cols)
            rope(h, parity, maps)
            ahead(first, 7, cols)

        dve.memset(zeros[:, :], 0.0).then_inc(zeroed, 1)
        dve.memset(minus_half, -0.5).then_inc(powers_ready, 1)
        dve.memset(eps_sum, HEAD_DIM * EPS).then_inc(powers_ready, 1)
        for k in range(SLOTS):
            split_x(k)
            split_unit(k, k, KU * HC)
        for k in range(SLOTS):
            split_x(SLOTS + k)
            ahead(0, k, KU * HC)
        dve.wait_ge(lam_loaded, 16 * 5)
        for n in range(2):
            dve.tensor_tensor(lam_prod[:, n, :], lam_in[:, 2 * n, :], lam_in[:, 2 * n + 1, :],
                              ALU.mult).then_inc(lam_mult, 1)
        dve.wait_ge(lam_mult, 2)
        for n in range(2):
            dve.reduce_sum(lam_sum[:, n:n + 1], lam_prod[:, n, :], AX.X).then_inc(lam_summed, 1)
        for k in range(SLOTS, UPH):
            if k == UPH - 1:
                dve.wait_ge(tables_loaded, 16)
                rope(0, 0, 2)
            ahead(0, k, KU * HC)
        dve.wait_ge(lam_exped, 1)
        dve.scalar_tensor_tensor(out=neg_lam, in0=lam_exp[:, 1:2], scalar=LAMBDA_INIT,
                                 in1=lam_exp[:, 0:1], op0=ALU.subtract,
                                 op1=ALU.subtract).then_inc(lam_ready, 1)
        dve.wait_ge(lam_ready, 1)
        slot(1, 1, 2, 2, 0)
        with dve.Fori(1, N_DIFF // 2) as j:
            slot(2 * j, 0, 2, 2, 2)
            slot(2 * j + 1, 1, 2, 2, 2)
        slot(N_DIFF, 0, 1, 2, 2)
        slot(N_DIFF + 1, 1, 1, 1, 2)
        with dve.Fori(N_DIFF // 2 + 1, HEADS // 2 - 1) as j:
            slot(2 * j, 0, 1, 1, 1)
            slot(2 * j + 1, 1, 1, 1, 1)
        slot(HEADS - 2, 0, 1, 1, 1)
        slot(HEADS - 1, 1, 1, 1, 1)

        def add_residual(n, y, tok_done, end, summed, tts=(0, 1)):
            for tt in tts:
                if tt == 0:
                    dve.wait_ge(tok_done, n + 1)
                else:
                    dve.wait_ge(w_used, end)
                cols = slice(n * NC, (n + 1) * NC) if isinstance(n, int) else bass.ds(n * NC, NC)
                dve.scalar_tensor_tensor(out=y[:, tt, cols], in0=y[:, tt, cols], scalar=ALPHA,
                                         in1=acc_ps[:, tt, :], op0=ALU.mult,
                                         op1=ALU.add).then_inc(summed, 1)

        def tok_stats(n, tt, y, summed, stat_done):
            dve.wait_ge(summed, TT * n + tt + 1)
            cols = slice(n * NC, (n + 1) * NC) if isinstance(n, int) else bass.ds(n * NC, NC)
            first = tt * CHUNKS * 6 + n * 6
            where = slice(first, first + 6) if isinstance(n, int) else bass.ds(first, 6)
            dve.bn_stats(stats[:, where], y[:, tt, cols]).then_inc(stat_done, 1)

        def tok_moments(tt, stat_done):
            dve.wait_ge(stat_done, TT * (CHUNKS - 1) + tt + 1)
            dve.bn_aggr(mean_var[:, 2 * tt:2 * tt + 2],
                        stats[:, tt * CHUNKS * 6:(tt + 1) * CHUNKS * 6]).then_inc(moments, 1)

        def centre(norm, tt, cols, y, gb):
            dve.wait_ge(moments, TT * norm + tt + 1)
            dve.scalar_tensor_tensor(out=y[:, tt, cols], in0=y[:, tt, cols],
                                     scalar=mean_var[:, 2 * tt:2 * tt + 1], in1=gb[:, 0, cols],
                                     op0=ALU.subtract, op1=ALU.mult).then_inc(centred, 1)

        def finish_norm(norm, count, tt, cols, y, gb, ready):
            dve.wait_ge(centred, count)
            dve.wait_ge(std_ready, TT * norm + tt + 1)
            dve.scalar_tensor_tensor(out=y[:, tt, cols], in0=y[:, tt, cols],
                                     scalar=inv_std[:, tt:tt + 1], in1=gb[:, 1, cols],
                                     op0=ALU.mult, op1=ALU.add).then_inc(ready, 1)

        split_mix(HEADS - 2, 1)
        ahead(U_OUT, 0)
        mask_and_max(HEADS - 1, 1)
        ahead(U_OUT, 1)
        ahead(U_OUT, 2)
        invert_sums(HEADS - 1, 1)
        combine(HEADS - 1, 1)
        ahead(U_OUT, 3)
        ahead(U_OUT, 4)
        split_mix(HEADS - 1, 1)
        ahead(U_OUT, 5)
        add_residual(0, y1, out_done, U_OUT + UPH, y1_summed)
        ahead(U_OUT, 6)
        ahead(U_OUT, 7)
        for tt in range(TT):
            tok_stats(0, tt, y1, y1_summed, y1_stats)
        with dve.Fori(1, CHUNKS - 1) as n:
            for k in range(UPH):
                if k == UPH - 2:
                    add_residual(n, y1, out_done, UPH * n + (U_OUT + UPH), y1_summed)
                ahead(UPH * n + U_OUT, k)
            for tt in range(TT):
                tok_stats(n, tt, y1, y1_summed, y1_stats)

        def sums_done(tt):
            add_residual(CHUNKS - 1, y1, out_done, U_FF1, y1_summed, (tt,))
            tok_stats(CHUNKS - 1, tt, y1, y1_summed, y1_stats)
            tok_moments(tt, y1_stats)

        def norm_piece(i):
            tt, c = PIECES[i]
            cols = slice(c * NC, (c + 1) * NC)
            centre(0, tt, cols, y1, ln1_gb)
            finish_norm(0, i + 1, tt, cols, y1, ln1_gb, x1_ready)

        def split_piece(i):
            tt, c = PIECES[i]
            dve.wait_ge(turn_rounded, UPH + i + 1)
            where = (slice(None), slice(c * TPC, (c + 1) * TPC), slice(tt * P, (tt + 1) * P))
            dve.tensor_tensor(x1T_lo[where], piece_ps[i % 4].rearrange("p (k t) -> p k t", k=TPC),
                              x1T_hi[where].bitcast(F32), ALU.subtract).then_inc(turn_split, 1)

        last_out = U_OUT + UPH * (CHUNKS - 1)

        def split_side(k):
            dve.wait_ge(side_rounded, k + 1)
            dve.tensor_tensor(side_lo[:, k, :], side_raw[:, k, :], side_hi[:, k, :].bitcast(F32),
                              ALU.subtract).then_inc(side_split, 1)

        ahead(last_out, 0)
        split_side(0)
        ahead(last_out, 1)
        for n in range(SPARE):
            split_spare(n, U_FF1 - SPARE + n, n + SLOTS - SPARE, spare_out_hi)
        for k in range(1, SLOTS):
            split_side(k)
        dve.wait_ge(gb1_loaded, 32)
        sums_done(0)
        norm_piece(0)
        norm_piece(1)
        split_piece(0)
        norm_piece(2)
        split_piece(1)
        ahead(U_FF1, 0, units=SLOTS + 1)
        sums_done(1)
        split_piece(2)
        norm_piece(3)
        ahead(U_FF1, 1)
        ahead(U_FF1, 2)
        split_piece(3)
        norm_piece(4)
        ahead(U_FF1, 3)
        norm_piece(5)
        split_piece(4)
        norm_piece(6)
        split_piece(5)
        norm_piece(7)
        split_piece(6)
        split_piece(7)

        def square_hidden(i):
            dve.wait_ge(relu_done, TT * i + TT)
            dve.tensor_tensor(relu[:, :, :], relu[:, :, :], relu[:, :, :], ALU.mult).then_inc(
                hid_squared, 1)

        def split_hidden(i, last=False):
            dve.wait_ge(hid_rounded, i + 1)
            hi = late_hi if last else hidT_hi[:, bass.ds(i * TPC, TPC), :]
            lo = late_lo if last else hidT_lo[:, bass.ds(i * TPC, TPC), :]
            dve.tensor_tensor(lo.rearrange("p k t -> p (k t)"),
                              scores_ps.rearrange("p b n -> p (b n)"),
                              hi.rearrange("p k t -> p (k t)").bitcast(F32),
                              ALU.subtract).then_inc(hid_split, 1)

        for k in range(SLOTS, UPH):
            ahead(U_FF1, k)
        square_hidden(0)
        dve.wait_ge(spilled, 16 * len(PIECES))
        with dve.Fori(1, CHUNKS_FF) as i:
            for k in range(UPH):
                if k == 2:
                    split_hidden(i - 1)
                ahead(UPH * i + U_FF1, k)
            square_hidden(i)

        for n in range(CHUNKS):
            first = U_FF2 + UPF * n
            if n == 0:
                for k in range(SLOTS):
                    if k == 2:
                        split_hidden(CHUNKS_FF - 1, last=True)
                    ahead(first, k)
            last = n == CHUNKS - 1
            with dve.Fori(SLOTS if n == 0 else 0, UPF - (2 if last else 1) * SLOTS, SLOTS) as k0:
                for k in range(SLOTS):
                    ahead(first + k0, k)
            if last:
                for k in range(SLOTS - SPARE):
                    ahead(U_END - 2 * SLOTS, k)
                for k in range(SPARE):
                    split_spare(k, U_END - SPARE + k, k + SLOTS - SPARE, spare_ff2_hi)
            else:
                if n == 0:
                    dve.wait_ge(x1_back, 16)
                for k in range(SLOTS):
                    if k == SLOTS - 2:
                        add_residual(n, y2, ff2_done, first + UPF, y2_summed)
                    ahead(first + UPF - SLOTS, k)
                for tt in range(TT):
                    tok_stats(n, tt, y2, y2_summed, y2_stats)

        dve.wait_ge(gb2_loaded, 32)
        count = len(PIECES)
        for tt in range(TT):
            add_residual(CHUNKS - 1, y2, ff2_done, U_END, y2_summed, (tt,))
            tok_stats(CHUNKS - 1, tt, y2, y2_summed, y2_stats)
            tok_moments(tt, y2_stats)
            pieces = [cols for t, cols in LAST_PIECES if t == tt]
            centre(1, tt, pieces[0], y2, ln2_gb)
            for cols, following in zip(pieces, pieces[1:] + [None]):
                if following is not None:
                    centre(1, tt, following, y2, ln2_gb)
                count += 1
                finish_norm(1, count, tt, cols, y2, ln2_gb, y2_ready)

    def gpsimd_program(pool):
        pool.wait_ge(powers_ready, 2)

        def rms_scale(h):
            pool.wait_ge(squared, h + 1)
            pool.tensor_tensor(mean_sq, sum_sq, eps_sum, ALU.add).then_inc(mean_ready, 1)
            pool.wait_ge(mean_ready, h + 1)
            pool.tensor_tensor(root, mean_sq, minus_half, ALU.pow).then_inc(root_ready, 1)
            pool.wait_ge(root_ready, h + 1)
            pool.tensor_tensor(o_scale, root, inv_sum[:, 0:4:2], ALU.mult).then_inc(scale_ready, 1)

        def norm_scale(norm):
            for tt in range(TT):
                n = TT * norm + tt + 1
                pool.wait_ge(moments, n)
                pool.tensor_scalar(var_eps[:, tt:tt + 1], mean_var[:, 2 * tt + 1:2 * tt + 2], EPS,
                                   None, ALU.add).then_inc(var_ready, 1)
                pool.wait_ge(var_ready, n)
                pool.tensor_tensor(inv_std[:, tt:tt + 1], var_eps[:, tt:tt + 1],
                                   minus_half[:, tt:tt + 1], ALU.pow).then_inc(std_ready, 1)

        pool.wait_ge(w_used, 2)
        for n, v in enumerate((lq1, lk1, lq2, lk2)):
            pool.dma_start(lam_in[:, n, :], v.partition_broadcast(P).rearrange(
                "p l d -> p (l d)")).then_inc(lam_loaded, 16)
        pool.dma_start(subln, subln_g.rearrange("l d -> d l")).then_inc(lam_loaded, 16)
        pool.dma_start(tables[:, :], table[:, P:T_COLS]).then_inc(tables_loaded, 16)
        with pool.Fori(0, N_DIFF) as h:
            rms_scale(h)
        for n, v in enumerate((ln1_g, ln1_b)):
            pool.wait_ge(lam_summed, 2)
            pool.dma_start(ln1_gb[:, n, :], v.partition_broadcast(P).rearrange(
                "p l d -> p (l d)")).then_inc(gb1_loaded, 16)
        norm_scale(0)
        for i, (tt, c) in enumerate(PIECES):
            cols = slice(c * NC, (c + 1) * NC)
            pool.wait_ge(x1_ready, i + 1)
            pool.dma_start(spill[:, tt, cols], y1[:, tt, cols]).then_inc(spilled, 16)
        pool.wait_ge(spilled, 16 * len(PIECES))
        pool.wait_ge(w_used, U_FF2)
        pool.dma_start(y2[:, :, :], spill).then_inc(x1_back, 16)
        norm_scale(1)

    with nc.Block() as block:
        @block.sync
        def _(sp):
            sp.dma_start(ident_t[:, :], table[:, 0:P]).then_inc(ident_loaded, 16)
            sync_program(sp)

        @block.tensor
        def _(pe):
            tensor_program(pe)

        @block.scalar
        def _(act):
            scalar_program(act)

        @block.vector
        def _(dve):
            vector_program(dve)

        @block.gpsimd
        def _(pool):
            gpsimd_program(pool)


_INS = ["x", "w_in", "lambda_q1", "lambda_k1", "lambda_q2", "lambda_k2", "subln_g", "w_out",
        "ln1_g", "ln1_b", "w_ff1", "w_ff2", "ln2_g", "ln2_b"]


def kernel(**inputs):
    import concourse.bacc as bacc
    from concourse.bass_utils import run_bass_kernel_spmd

    nc = bacc.Bacc("TRN2", target_bir_lowering=False, num_devices=1)
    arrays = {f"in_{n}": np.ascontiguousarray(inputs[n]) for n in _INS}
    arrays["in_table"] = constant_table()
    args = [nc.dram_tensor(n, a.shape, mybir.dt.from_np(a.dtype), kind="ExternalInput").ap()
            for n, a in arrays.items()]
    out = nc.dram_tensor("out_0", inputs["x"].shape, F32, kind="ExternalOutput").ap()
    hybrid_layer(nc, *args, out)
    result = run_bass_kernel_spmd(nc, [arrays], core_ids=[0])
    return result.results[0]["out_0"]
```
